# Optimizing a Trainium2 kernel written in Bass

```python
import math
import jax, jax.numpy as jnp
from jax import lax
import numpy as np

D_MODEL = 1024
BATCH = 1
SEQ = 512
DEPTH = 1

MIX_WIDTH = D_MODEL
GLA_HEADS = 4
GLA_DK = D_MODEL // 16
GLA_DV = D_MODEL // 8
GLA_KEY_WIDTH = GLA_HEADS * GLA_DK
GLA_WIDTH = GLA_HEADS * GLA_DV
GLA_GATE_RANK = 16
GLA_GATE_TEMP = 16.0
GLA_CHUNK = 64
SB_HEADS = 8
SB_DH = 64
SB_WIDTH = SB_HEADS * SB_DH
SB_BLOCK = 128
PEER_HEADS = 8
PEER_NKEYS = 128
PEER_NEXPERTS = PEER_NKEYS * PEER_NKEYS
PEER_QDIM = 256
PEER_HALF = PEER_QDIM // 2
PEER_TOPK = 16
PEER_TOKEN_BLOCK = 128
ALPHA = (2.0 * DEPTH) ** 0.25
BETA = (8.0 * DEPTH) ** -0.25
EPS = 1e-5

SPLIT_NAMES = ('q_gla', 'k_gla', 'v_gla', 'g_gla', 'a_gla', 'q_sb', 'k_sb', 'v_sb')
SPLIT_SIZES = (GLA_KEY_WIDTH, GLA_KEY_WIDTH, GLA_WIDTH, GLA_WIDTH, GLA_GATE_RANK,
               SB_WIDTH, SB_WIDTH, SB_WIDTH)
IN_WIDTH = sum(SPLIT_SIZES)
SPLIT_POINTS = [int(v) for v in np.cumsum(SPLIT_SIZES)[:-1]]

kernel_name = 'hybrid_gla_stickbreak_peer_deepnorm'

def layer_norm(x, g, b):
    xf = x.astype(jnp.float32)
    mu = jnp.mean(xf, axis=-1, keepdims=True)
    var = jnp.mean(jnp.square(xf - mu), axis=-1, keepdims=True)
    return ((xf - mu) * lax.rsqrt(var + EPS) * g + b).astype(x.dtype)

def rms_norm(x, g):
    xf = x.astype(jnp.float32)
    return (xf * lax.rsqrt(jnp.mean(xf * xf, axis=-1, keepdims=True) + EPS) * g).astype(x.dtype)

def gla_mixer(q, k, v, log_a):
    B, S = q.shape[0], q.shape[1]
    nc = S // GLA_CHUNK
    f32 = jnp.float32

    def to_chunks(t):
        return t.reshape(B, nc, GLA_CHUNK, t.shape[2], t.shape[3]).transpose(1, 0, 3, 2, 4).astype(f32)

    q, k, v, log_a = to_chunks(q) * (GLA_DK ** -0.5), to_chunks(k), to_chunks(v), to_chunks(log_a)
    b = jnp.cumsum(log_a, axis=-2)
    b_last = b[..., -1:, :]
    q_in = q * jnp.exp(b)
    k_in = k * jnp.exp(-b)
    k_state = k * jnp.exp(b_last - b)
    decay = jnp.exp(b_last)[..., 0, :, None]

    causal = jnp.tril(jnp.ones((GLA_CHUNK, GLA_CHUNK), dtype=bool))
    att = jnp.where(causal, jnp.einsum('nbhcd,nbhjd->nbhcj', q_in, k_in), 0.0)
    o_intra = jnp.einsum('nbhcj,nbhje->nbhce', att, v)

    def step(state, inp):
        qi, ks, vi, dec = inp
        o_inter = jnp.einsum('bhcd,bhde->bhce', qi, state)
        state = state * dec + jnp.einsum('bhjd,bhje->bhde', ks, vi)
        return state, o_inter

    state0 = jnp.zeros((B, q.shape[2], GLA_DK, GLA_DV), f32)
    _, o_inter = lax.scan(step, state0, (q_in, k_state, v, decay))
    o = o_intra + o_inter
    return o.transpose(1, 0, 3, 2, 4).reshape(B, S, GLA_HEADS, GLA_DV)

def stick_breaking(q, k, v):
    B, S, H, D = q.shape
    nb = S // SB_BLOCK
    scale = D ** -0.5
    qb = q.reshape(B, nb, SB_BLOCK, H, D).transpose(1, 0, 3, 2, 4)
    kT = k.transpose(0, 2, 1, 3)
    vT = v.transpose(0, 2, 1, 3)
    key_pos = jnp.arange(S)

    def block(args):
        qi, blk = args
        q_pos = blk * SB_BLOCK + jnp.arange(SB_BLOCK)
        z = jnp.einsum('bhqd,bhsd->bhqs', qi, kT).astype(jnp.float32) * scale
        mask = key_pos[None, :] < q_pos[:, None]
        log_not_break = jnp.where(mask, jax.nn.log_sigmoid(-z), 0.0)
        tail = lax.cumsum(log_not_break, axis=3, reverse=True) - log_not_break
        w = jnp.where(mask, jnp.exp(jax.nn.log_sigmoid(z) + tail), 0.0)
        return jnp.einsum('bhqs,bhsd->bhqd', w.astype(vT.dtype), vT)

    o = lax.map(block, (qb, jnp.arange(nb)))
    return o.transpose(1, 0, 3, 2, 4).reshape(B, S, H, D)

def hybrid_mixer(x, w_in, w_gla_gate, b_gla_gate, gla_norm_g, sb_norm_g, w_out):
    B, S, _ = x.shape
    proj = x @ w_in
    q_g, k_g, v_g, g_g, a_lr, q_s, k_s, v_s = jnp.split(proj, SPLIT_POINTS, axis=-1)

    log_a = jax.nn.log_sigmoid((a_lr @ w_gla_gate + b_gla_gate).astype(jnp.float32)) / GLA_GATE_TEMP
    o_gla = gla_mixer(q_g.reshape(B, S, GLA_HEADS, GLA_DK),
                      k_g.reshape(B, S, GLA_HEADS, GLA_DK),
                      v_g.reshape(B, S, GLA_HEADS, GLA_DV),
                      log_a.reshape(B, S, GLA_HEADS, GLA_DK))
    o_gla = rms_norm(o_gla, gla_norm_g).reshape(B, S, GLA_WIDTH).astype(x.dtype) * jax.nn.silu(g_g)

    o_sb = stick_breaking(q_s.reshape(B, S, SB_HEADS, SB_DH),
                          k_s.reshape(B, S, SB_HEADS, SB_DH),
                          v_s.reshape(B, S, SB_HEADS, SB_DH))
    o_sb = rms_norm(o_sb, sb_norm_g).reshape(B, S, SB_WIDTH).astype(x.dtype)

    return jnp.concatenate([o_gla, o_sb], axis=-1) @ w_out

def peer_ffn(x, w_query, sub_keys, expert_u, expert_v):
    B, S, D = x.shape
    T = B * S
    xt = x.reshape(T, D)
    qry = (xt @ w_query).reshape(T, PEER_HEADS, 2, PEER_HALF)
    scores = jnp.einsum('thpc,hpnc->thpn', qry, sub_keys).astype(jnp.float32)
    s_top, i_top = lax.top_k(scores, PEER_TOPK)
    cand = (s_top[:, :, 0, :, None] + s_top[:, :, 1, None, :]).reshape(T, PEER_HEADS, PEER_TOPK * PEER_TOPK)
    cand_idx = (i_top[:, :, 0, :, None] * PEER_NKEYS + i_top[:, :, 1, None, :]).reshape(T, PEER_HEADS, PEER_TOPK * PEER_TOPK)
    best, pos = lax.top_k(cand, PEER_TOPK)
    idx = jnp.take_along_axis(cand_idx, pos, axis=-1)
    gate = jax.nn.softmax(best, axis=-1)
    HK = PEER_HEADS * PEER_TOPK
    nb = T // PEER_TOKEN_BLOCK

    def block(args):
        xb, ib, gb = args
        u = expert_u[ib]
        h = jax.nn.gelu(jnp.einsum('tkd,td->tk', u, xb).astype(jnp.float32), approximate=False)
        vsel = expert_v[ib]
        return jnp.einsum('tk,tkd->td', (gb * h).astype(xb.dtype), vsel)

    out = lax.map(block, (xt.reshape(nb, PEER_TOKEN_BLOCK, D),
                          idx.reshape(nb, PEER_TOKEN_BLOCK, HK),
                          gate.reshape(nb, PEER_TOKEN_BLOCK, HK)))
    return out.reshape(B, S, D)

def setup_inputs(seed: int = 0) -> dict:
    key = jax.random.key(seed)
    ks = jax.random.split(key, 16)
    L, D = DEPTH, D_MODEL
    f32 = jnp.float32

    def nrm(k, shape, scale):
        return jax.random.normal(k, shape, f32) * scale

    col_scale = np.concatenate([np.full((s,), BETA if n in ('v_gla', 'v_sb') else 1.0, np.float32)
                                for n, s in zip(SPLIT_NAMES, SPLIT_SIZES)])
    return {
        'x': nrm(ks[0], (BATCH, SEQ, D), 1.0),
        'w_in': nrm(ks[1], (L, D, IN_WIDTH), D ** -0.5) * jnp.asarray(col_scale),
        'w_gla_gate': nrm(ks[2], (L, GLA_GATE_RANK, GLA_KEY_WIDTH), GLA_GATE_RANK ** -0.5),
        'b_gla_gate': nrm(ks[3], (L, GLA_KEY_WIDTH), 0.1),
        'gla_norm_g': 1.0 + nrm(ks[4], (L, GLA_HEADS, GLA_DV), 0.02),
        'sb_norm_g': 1.0 + nrm(ks[5], (L, SB_HEADS, SB_DH), 0.02),
        'w_out': nrm(ks[6], (L, MIX_WIDTH, D), MIX_WIDTH ** -0.5 * BETA),
        'ln1_g': 1.0 + nrm(ks[7], (L, D), 0.02),
        'ln1_b': nrm(ks[8], (L, D), 0.02),
        'peer_w_query': nrm(ks[9], (L, D, PEER_HEADS * PEER_QDIM), D ** -0.5),
        'peer_sub_keys': nrm(ks[10], (L, PEER_HEADS, 2, PEER_NKEYS, PEER_HALF), PEER_HALF ** -0.5),
        'peer_u': nrm(ks[11], (L, PEER_NEXPERTS, D), D ** -0.5 * BETA),
        'peer_v': nrm(ks[12], (L, PEER_NEXPERTS, D), BETA),
        'ln2_g': 1.0 + nrm(ks[13], (L, D), 0.02),
        'ln2_b': nrm(ks[14], (L, D), 0.02),
    }

def reference(x, w_in, w_gla_gate, b_gla_gate, gla_norm_g, sb_norm_g, w_out, ln1_g, ln1_b,
              peer_w_query, peer_sub_keys, peer_u, peer_v, ln2_g, ln2_b):
    for l in range(DEPTH):
        mix = hybrid_mixer(x, w_in[l], w_gla_gate[l], b_gla_gate[l], gla_norm_g[l], sb_norm_g[l], w_out[l])
        x = layer_norm(ALPHA * x + mix, ln1_g[l], ln1_b[l])
        ffn = peer_ffn(x, peer_w_query[l], peer_sub_keys[l], peer_u[l], peer_v[l])
        x = layer_norm(ALPHA * x + ffn, ln2_g[l], ln2_b[l])
    return x


_drawn_inputs = setup_inputs


def setup_inputs(seed=0):
    import zlib

    import numpy as np

    out = dict(_drawn_inputs(seed))
    spreads = {}
    factors = {'b_gla_gate': 3.794,
     'gla_norm_g': 5.589,
     'sb_norm_g': 4.015,
     'ln2_g': 2.741,
     'ln2_b': 2.874}
    for name, (base, spread) in spreads.items():
        noise = np.random.default_rng([zlib.crc32(name.encode()), seed]).standard_normal(out[name].shape)
        drawn = base * np.exp(spread * noise) if base else spread * noise
        out[name] = __import__('jax').numpy.asarray(drawn.astype(out[name].dtype))
    for name, factor in factors.items():
        out[name] = (out[name] * factor).astype(out[name].dtype)
    return out
```

```python
from contextlib import ExitStack

import concourse.bass as bass
from concourse import mybir

F32 = mybir.dt.float32
U32 = mybir.dt.uint32
ALU = mybir.AluOpType
ACT = mybir.ActivationFunctionType
AX_X = mybir.AxisListType.X

P = 128
D = 1024
SEQ = 512
NB = SEQ // P
KC = D // P
GH, GDK, GDV, GC = 4, 64, 128, 64
RANK = 16
GATE_TEMP = 16.0
SH, SD = 8, 64
PH, NKEYS, TOPK = 8, 128, 16
QW = 2 * P
SLOTS = PH * TOPK
ALPHA = 2.0 ** 0.25
EPS = 1e-5
LOWEST = -3.0e38

RING = 8
GROUP = 4
GROUPS = TOPK // GROUP

C_QK, C_VG, C_GG, C_A, C_QS, C_KS, C_VS = 0, 512, 1024, 1536, 1552, 2064, 2576
W_GROUPS = [C_QK, C_VG, C_GG, C_QS, C_KS, C_VS]
WBUFS = 3


class Steps:

    def __init__(self, eng, sem):
        self.eng, self.sem, self.n = eng, sem, 0

    def __call__(self, ins):
        self.n += 1
        ins.then_inc(self.sem, 1)

    def wait(self):
        self.eng.wait_ge(self.sem, self.n)

    def restart(self):
        if self.n:
            self.wait()
        self.eng.sem_clear(self.sem)
        self.n = 0


def hybrid_layer(nc, x, xT, w_in, w_gate, b_gate, gains, w_out, ln, w_query, keysT, experts, out):
    ctx = ExitStack()
    with ctx:
        def sb(name, shape, dt=F32):
            return ctx.enter_context(nc.sbuf_tensor(name, shape, dt))

        def sem(name):
            return ctx.enter_context(nc.semaphore(name))

        bank = [ctx.enter_context(nc.psum_tensor(f"bank{i}", [P, 512], F32)) for i in range(8)]

        x_sb = sb("x_sb", [P, NB, D])
        x1T = sb("x1T", [P, KC, P])
        ln_sb = sb("ln_sb", [P, 4, D])
        gains_sb = sb("gains_sb", [P, D])
        ring = sb("ring", [P, RING * 2 * D])
        big = sb("big", [P, KC * PH * QW])
        keys = sb("keys", [P, 2 * PH * NKEYS])
        scr = sb("scr", [P, 6144])
        ident = sb("ident", [P, P])
        neg_tri = sb("neg_tri", [P, P])
        neg_one = sb("neg_one", [P, P])
        before = sb("before", [P, P])
        chunk_mask = sb("chunk_mask", [P, P])
        carry = sb("carry", [P, SEQ])
        iota16 = sb("iota16", [P, TOPK])
        bg_sb = sb("bg_sb", [P, 2])
        stats = sb("stats", [P, 2, 6])
        mv = sb("mv", [P, 2])
        rstd = sb("rstd", [P, 1])
        ms = sb("ms", [P, GH + SH])

        xT_sb = ring[:, 0:KC * SEQ].rearrange("p (k t) -> p k t", k=KC)
        w_buf = [ring[:, (i + 1) * 4096:(i + 2) * 4096].rearrange("p (k n) -> p k n", k=KC)
                 for i in range(WBUFS)]
        wa_sb = scr[:, 4096:4096 + KC * RANK].rearrange("p (k n) -> p k n", k=KC)
        wg_sb = scr[0:RANK, 4096 + KC * RANK:4096 + KC * RANK + 256]
        qgT = big[:, 0:1024].rearrange("p (h t) -> p h t", h=2)
        kgT = big[:, 1024:2048].rearrange("p (h t) -> p h t", h=2)
        qsT = big[:, 2048:4096].rearrange("p (h t) -> p h t", h=4)
        ksT = big[:, 4096:6144].rearrange("p (h t) -> p h t", h=4)
        vg = big[:, 6144:8192].rearrange("p (b n) -> p b n", b=NB)
        gg = big[:, 8192:10240].rearrange("p (b n) -> p b n", b=NB)
        vs = big[:, 10240:12288].rearrange("p (b n) -> p b n", b=NB)
        aT = big[0:RANK, 12288:12800]
        kin = big[:, 12800:13824].rearrange("p (h t) -> p h t", h=2)
        oT = big[:, 13824:14848].rearrange("p (k t) -> p k t", k=KC)
        attm = big[:, 14848:15360].rearrange("p (r h t) -> p r h t", r=2, h=2)
        wo_sb = ring[:, 0:8192].rearrange("p (k n) -> p k n", k=KC)
        wT = ring[:, 8192:12288].rearrange("p (r c n) -> p r c n", r=2, c=NB)
        sp = ring[:, 12288:16384].rearrange("p (r c n) -> p r c n", r=2, c=NB)
        o_n = keys[:, 0:1024]
        kstT = keys[:, 1024:2048].rearrange("p (b h n) -> p b h n", b=NB, h=2)
        cum = scr[:, 0:1024].rearrange("p (h t) -> p h t", h=2)
        ecum = scr[:, 1024:2048].rearrange("p (h t) -> p h t", h=2)
        t1 = scr[:, 2048:3072].rearrange("p (h t) -> p h t", h=2)
        t2 = scr[:, 3072:4096].rearrange("p (h t) -> p h t", h=2)
        state = scr[:, 4096:6144].rearrange("p (c h n) -> p c h n", c=8, h=2)
        lse = scr[:, 0:2048].rearrange("p (c n) -> p c n", c=NB)
        zmin = scr[:, 2048:2560]
        sq = scr[:, 2560:3584]
        egate = scr[:, 3584:4096]
        wq_sb = big[:, :].rearrange("p (k n) -> p k n", k=KC)
        rows = [ring[:, i * 2 * D:(i + 1) * 2 * D] for i in range(RING)]
        q_sb = scr[:, 0:256]
        qT_sb = scr[:, 256:512].rearrange("p (s t) -> p s t", s=2)
        sc = scr[:, 512:768].rearrange("p (s n) -> p s n", s=2)
        sc2 = scr[:, 768:1024].rearrange("p (s n) -> p s n", s=2)
        cand = scr[:, 1024:1280]
        cand2 = scr[:, 1280:1536]
        onehot = scr[:, 1536:2048].rearrange("p (s k a) -> p s k a", s=2, k=TOPK)
        diag = scr[:, 2048:3072].rearrange("p (s n) -> p s n", s=RING)
        gates = scr[:, 3072:3328]
        top = scr[:, 3328:3360].rearrange("p (s k) -> p s k", s=2)
        topf = scr[:, 3360:3392].rearrange("p (s k) -> p s k", s=2)
        posf = scr[:, 3392:3424].rearrange("p (s k) -> p s k", s=2)
        sel = scr[:, 3424:3456].rearrange("p (s k) -> p s k", s=2)
        best = scr[:, 3456:3472]
        eb = scr[:, 3472:3488]
        nbest = scr[:, 3488:3489]
        esum = scr[:, 3489:3490]
        gate_now = scr[:, 3496:3512]
        dots = scr[:, 3512:3520].rearrange("p (s k) -> p s k", s=2)
        acts = scr[:, 3520:3528].rearrange("p (s k) -> p s k", s=2)
        wts = scr[:, 3528:3536].rearrange("p (s k) -> p s k", s=2)
        y2 = scr[:, 4096:5120]
        zeros = scr[:, 5120:5632]
        topi = sb("topi", [P, 2, TOPK], U32)
        pos = sb("pos", [P, 2, TOPK], U32)
        idx = sb("idx", [P, 2 * SLOTS], U32)
        idx_now = sb("idx_now", [P, 2, GROUP], U32)

        xT_in, wa_in, x_in, consts_in, wo_in, wq_in, keys_in = (
            sem(n) for n in ("xT_in", "wa_in", "x_in", "consts_in", "wo_in", "wq_in", "keys_in"))
        w_in_sem = [sem(f"w_in{i}") for i in range(WBUFS)]
        made, filled = sem("made"), sem("filled")
        proj_group, proj_tile, ev_act, ev_dve = (sem(n) for n in ("proj_group", "proj_tile", "ev_act", "ev_dve"))
        act_steps, dve_steps, pool_steps = (sem(n) for n in ("act_steps", "dve_steps", "pool_steps"))
        u_ready, uabs, umin, uexp, cumd, ecumd, kst_exp, dlast, qk_ready, kst_T, kst_copied, su_ready, st_ready = (
            sem(n) for n in ("u_ready", "uabs", "umin", "uexp", "cumd", "ecumd", "kst_exp", "dlast", "qk_ready",
                             "kst_T", "kst_copied", "su_ready", "st_ready"))
        z_ready, l_ready, sp_ready, zc_ready, zmin_ready, w_exp, w_masked, att_ready, attm_ready, av_ready, go_ready = (
            sem(n) for n in ("z_ready", "l_ready", "sp_ready", "zc_ready", "zmin_ready", "w_exp", "w_masked",
                             "att_ready", "attm_ready", "av_ready", "go_ready"))
        o_copied, ms_ready, rs_ready, eg_ready, on_ready, oT_ready, oT_copied, mix_ready, var1, rstd1, x1_ready = (
            sem(n) for n in ("o_copied", "ms_ready", "rs_ready", "eg_ready", "on_ready", "oT_ready", "oT_copied",
                             "mix_ready", "var1", "rstd1", "x1_ready"))
        x1T_done, x1T_copied, q_done, q_copied, qT_done, qT_copied, sc_done, sc_copied, best_ready, gexp, routed = (
            sem(n) for n in ("x1T_done", "x1T_copied", "q_done", "q_copied", "qT_done", "qT_copied", "sc_done",
                             "sc_copied", "best_ready", "gexp", "routed"))
        landed = [sem(f"landed{i}") for i in range(RING)]
        dot_done, gelu_done, w_done, diag_done, v_done, ffn_done, var2, rstd2, y_ready, stored = (
            sem(n) for n in ("dot_done", "gelu_done", "w_done", "diag_done", "v_done", "ffn_done", "var2", "rstd2",
                             "y_ready", "stored"))

        tiles = []
        for g, c in enumerate(W_GROUPS):
            for j in range(4):
                if c == C_QK:
                    tiles.append((g, "w", j, (qgT, kgT)[j // 2][:, j % 2, :], 1.0))
                elif c == C_QS:
                    tiles.append((g, "w", j, qsT[:, j, :], SD ** -0.5))
                elif c == C_KS:
                    tiles.append((g, "w", j, ksT[:, j, :], 1.0))
                else:
                    tiles.append((g, "x", j, {C_VG: vg, C_GG: gg, C_VS: vs}[c][:, j, :], 1.0))
            if g == 0:
                tiles.append((0, "a", 0, aT, 1.0))
        NT = len(tiles)

        block = ctx.enter_context(nc.Block())

        def zi(b, par, c):
            return sum(2 * (i + 1) for i in range(b)) + par * (b + 1) + (b - c)

        ZB = 4
        units = lambda b, h: b * PH + h

        @block.sync
        def _(sp_eng):
            xT_v = xT.rearrange("(k p) t -> p k t", p=P)
            w_v = w_in.rearrange("(k p) n -> p k n", p=P)
            sp_eng.dma_start(xT_sb, xT_v).then_inc(xT_in, 16)
            for g, c in enumerate(W_GROUPS):
                if g >= WBUFS:
                    sp_eng.wait_ge(proj_group, g - WBUFS + 1)
                sp_eng.dma_start(w_buf[g % WBUFS], w_v[:, :, c:c + 512]).then_inc(w_in_sem[g % WBUFS], 16)
                if g == 0:
                    with nc.allow_non_contiguous_dma(reason="16 columns"):
                        sp_eng.dma_start(wa_sb, w_v[:, :, C_A:C_A + RANK]).then_inc(wa_in, 16)
                    sp_eng.dma_start(wg_sb, w_gate).then_inc(wa_in, 16)
                    sp_eng.dma_start(bg_sb[:], b_gate).then_inc(wa_in, 16)
            sp_eng.dma_start(x_sb[:], x.rearrange("(b p) d -> p b d", p=P)).then_inc(x_in, 16)
            sp_eng.dma_start(gains_sb[:], gains.partition_broadcast(P)).then_inc(consts_in, 16)
            for i in range(4):
                sp_eng.dma_start(ln_sb[:, i, :], ln[i:i + 1, :].rearrange("a d -> (a d)").partition_broadcast(P)).then_inc(consts_in, 16)
            sp_eng.wait_ge(proj_group, len(W_GROUPS))
            sp_eng.dma_start(wo_sb, w_out.rearrange("(k p) n -> p k n", p=P)).then_inc(wo_in, 16)
            sp_eng.wait_ge(mix_ready, NB)
            sp_eng.dma_start(keys[:], keysT).then_inc(keys_in, 16)
            sp_eng.dma_start(wq_sb, w_query.rearrange("(k p) n -> p k n", p=P)).then_inc(wq_in, 16)
            out_v = out.rearrange("(b p) d -> b p d", p=P)
            for b in range(NB):
                sp_eng.wait_ge(y_ready, b + 1)
                sp_eng.dma_start(out_v[b], y2).then_inc(stored, 16)
            sp_eng.wait_ge(stored, 16 * NB)

        @block.gpsimd
        def _(pool):
            g = nc.gpsimd
            st = Steps(pool, pool_steps)
            g.memset(ident[:], 0.0)
            g.memset(neg_one[:], -1.0)
            g.memset(neg_tri[:], -1.0)
            g.memset(before[:], 1.0)
            g.memset(chunk_mask[:], 1.0)
            g.memset(carry[:], 1.0)
            st(g.iota(iota16[:], [[1, TOPK]], base=0, channel_multiplier=0, allow_small_or_imprecise_dtypes=True))
            st.wait()
            g.affine_select(out=ident[:], in_=ident[:], compare_op=ALU.not_equal, fill=1.0, base=0,
                            pattern=[[-1, P]], channel_multiplier=1)
            g.affine_select(out=neg_tri[:], in_=neg_tri[:], compare_op=ALU.is_ge, fill=0.0, base=0,
                            pattern=[[-1, P]], channel_multiplier=1)
            g.affine_select(out=before[:], in_=before[:], compare_op=ALU.is_gt, fill=0.0, base=0,
                            pattern=[[1, P]], channel_multiplier=-1)
            g.memset(carry[:, :].rearrange("p (c t) -> p c t", t=GC)[:, :, 0:1], 0.0)
            st(g.affine_select(out=chunk_mask[:], in_=chunk_mask[:], compare_op=ALU.is_ge, fill=0.0, base=0,
                               pattern=[[1, P]], channel_multiplier=-1))
            st.wait()
            g.affine_select(out=chunk_mask[:, GC:P], in_=chunk_mask[:, GC:P], compare_op=ALU.is_ge, fill=0.0, base=-GC,
                            pattern=[[0, GC]], channel_multiplier=1).then_inc(made, 1)
            for b in range(NB):
                st.restart()
                with pool.Fori(0, PH) as h:
                    for grp in range(GROUPS):
                        half = grp % 2
                        if grp == 0:
                            pool.wait_ge(routed, h + (b * PH + 1))
                        pool.wait_ge(v_done, h * GROUPS + (b * PH * GROUPS + grp + 1))
                        st(g.tensor_copy(idx_now[:, half, :], idx[:, bass.ds(h * TOPK + ((b % 2) * SLOTS + grp * GROUP), GROUP)]))
                        st.wait()
                        for k in range(GROUP):
                            s = half * GROUP + k
                            g.indirect_dma_start(rows[s], None, experts, bass.IndirectOffsetOnAxis(
                                ap=idx_now[:, half, k:k + 1], axis=0)).then_inc(landed[s], 16)
                    st.restart()

        @block.tensor
        def _(pe):
            t = nc.tensor
            pe.wait_ge(xT_in, 16)
            for i, (grp, side, j, _, _) in enumerate(tiles):
                if side == "a":
                    pe.wait_ge(wa_in, 48)
                elif j == 0:
                    pe.wait_ge(w_in_sem[grp % WBUFS], 16 * (grp // WBUFS + 1))
                if i >= 8:
                    pe.wait_ge((ev_act, ev_dve)[i % 2], (i - 8) // 2 + 1)
                w = w_buf[grp % WBUFS]
                for k in range(KC):
                    if side == "w":
                        mm = t.matmul(bank[i % 8][:], w[:, k, j * P:(j + 1) * P], xT_sb[:, k, :], start=k == 0, stop=k == KC - 1)
                    elif side == "x":
                        mm = t.matmul(bank[i % 8][:], xT_sb[:, k, j * P:(j + 1) * P], w[:, k, :], start=k == 0, stop=k == KC - 1)
                    else:
                        mm = t.matmul(bank[i % 8][0:RANK, :], wa_sb[:, k, :], xT_sb[:, k, :], start=k == 0, stop=k == KC - 1)
                mm.then_inc(proj_tile, 1)
                if i + 1 == NT or (tiles[i + 1][0] != grp):
                    pe.wait_ge(proj_tile, i + 1)
                    pe.sem_inc(proj_group, 1)

            pe.wait_ge(ev_act, (NT + 1) // 2)
            pe.wait_ge(ev_dve, NT // 2)
            for hp in range(2):
                t.matmul(bank[hp][:], wg_sb[:, hp * P:(hp + 1) * P], aT, start=True, stop=True).then_inc(u_ready, 1)
            pe.wait_ge(qk_ready, 1)
            pe.wait_ge(made, 1)
            for b in range(NB):
                for hp in range(2):
                    i = 2 * b + hp
                    mm = t.transpose(bank[2 + i // 4][:, (i % 4) * P:(i % 4 + 1) * P], kgT[:, hp, b * P:(b + 1) * P], ident[:])
                    if i % 4 == 3:
                        mm.then_inc(kst_T, 1)
            pe.wait_ge(kst_copied, 2)
            for c in range(7):
                if c >= 4:
                    pe.wait_ge(st_ready, c - 3)
                b, r = c // 2, (c % 2) * GC
                for h in range(GH):
                    hp, q = h // 2, (h % 2) * GDK
                    mm = t.matmul(bank[4 + c % 4][q:q + GDK, hp * GDV:(hp + 1) * GDV], kstT[r:r + GC, b, hp, q:q + GDK],
                                  vg[r:r + GC, b, h * GDV:(h + 1) * GDV], start=True, stop=True)
                mm.then_inc(su_ready, 1)

            for b in range(NB):
                for par in range(2):
                    r = par * SD
                    for c in range(b, -1, -1):
                        n = zi(b, par, c)
                        z = bank[n % ZB]
                        if n < ZB:
                            pe.wait_ge(st_ready, 7)
                        else:
                            pe.wait_ge(w_exp, n - ZB + 1)
                        for j in range(4):
                            mm = t.matmul(z[:, j * P:(j + 1) * P], ksT[r:r + SD, j, c * P:(c + 1) * P],
                                          qsT[r:r + SD, j, b * P:(b + 1) * P], start=j == 0, stop=False, skip_group_check=True)
                        mm.then_inc(z_ready, 1)
                    for c in range(b, -1, -1):
                        n = zi(b, par, c)
                        pe.wait_ge(sp_ready, n + 1)
                        for c2 in range(b, c, -1):
                            t.matmul(bank[n % ZB][:], neg_one[:], sp[:, par, c2, :], start=False, stop=False, skip_group_check=True)
                        t.matmul(bank[n % ZB][:], neg_tri[:], sp[:, par, c, :], start=False, stop=True,
                                 skip_group_check=True).then_inc(zc_ready, 1)
                if b:
                    pe.wait_ge(x1_ready, b)
                for h in range(GH):
                    hp, par = h // 2, h % 2
                    q = par * GDK
                    mm = t.matmul(bank[5 + par][:, hp * P:(hp + 1) * P], kin[q:q + GDK, hp, b * P:(b + 1) * P],
                                  qgT[q:q + GDK, hp, b * P:(b + 1) * P], start=True, stop=True)
                mm.then_inc(att_ready, 1)
                pe.wait_ge(w_exp, zi(b, 1, 0) + 1)
                pe.wait_ge(w_masked, 2 * (b + 1))
                for h in range(SH):
                    j, par = h // 2, h % 2
                    for c in range(b + 1):
                        mm = t.matmul(bank[4][:, h * SD:(h + 1) * SD], wT[:, par, c, j * P:(j + 1) * P],
                                      vs[:, c, h * SD:(h + 1) * SD], start=c == 0, stop=c == b)
                mm.then_inc(av_ready, 1)
                pe.wait_ge(attm_ready, b + 1)
                for h in range(GH):
                    hp, par = h // 2, h % 2
                    q, ob = par * GDK, bank[7 if par == 0 else 5]
                    mm = t.matmul(ob[:, hp * GDV:(hp + 1) * GDV], attm[:, par, hp, :], vg[:, b, h * GDV:(h + 1) * GDV],
                                  start=True, stop=False, skip_group_check=True)
                    for r in range(2):
                        c = 2 * b + r
                        if c:
                            mm = t.matmul(ob[r * GC:(r + 1) * GC, hp * GDV:(hp + 1) * GDV],
                                          qgT[q:q + GDK, hp, c * GC:(c + 1) * GC], state[q:q + GDK, c, hp, :],
                                          start=False, stop=True, skip_group_check=True)
                mm.then_inc(go_ready, 1)
                pe.wait_ge(on_ready, b + 1)
                for k in range(KC):
                    mm = t.transpose(bank[6 + k // 4][:, (k % 4) * P:(k % 4 + 1) * P], o_n[:, k * P:(k + 1) * P], ident[:])
                    if k % 4 == 3:
                        mm.then_inc(oT_ready, 1)
                pe.wait_ge(oT_copied, 2 * (b + 1))
                pe.wait_ge(wo_in, 16)
                for n in range(2):
                    for k in range(KC):
                        mm = t.matmul(bank[4 + n][:], oT[:, k, :], wo_sb[:, k, n * 512:(n + 1) * 512], start=k == 0, stop=k == KC - 1)
                mm.then_inc(mix_ready, 1)

            def transpose_x1(b):
                pe.wait_ge(x1_ready, b + 1)
                pe.wait_ge(sc_copied, b * PH + 1)
                for k in range(KC):
                    mm = t.transpose(bank[6 + k // 4][:, (k % 4) * P:(k % 4 + 1) * P], x_sb[:, b, k * P:(k + 1) * P], ident[:])
                mm.then_inc(x1T_done, 1)
                pe.wait_ge(x1T_copied, b + 1)

            def query(h, u0):
                u = h + u0
                for k in range(KC):
                    mm = t.matmul(bank[4][:, 0:QW], x1T[:, k, :], wq_sb[:, k, bass.ds(h * QW, QW)], start=k == 0, stop=k == KC - 1)
                mm.then_inc(q_done, 1)

            def query_T(h, u0):
                pe.wait_ge(q_copied, h + (u0 + 1))
                for s in range(2):
                    mm = t.transpose(bank[5][:, s * P:(s + 1) * P], q_sb[:, s * P:(s + 1) * P], ident[:])
                mm.then_inc(qT_done, 1)

            def scores(h, u0):
                pe.wait_ge(qT_copied, h + (u0 + 1))
                pe.wait_ge(sc_copied, h + (u0 + 1))
                for s in range(2):
                    mm = t.matmul(bank[6][:, s * P:(s + 1) * P], qT_sb[:, s, :], keys[:, bass.ds(h * QW + s * P, P)], start=True, stop=True)
                mm.then_inc(sc_done, 1)

            def values(h, b, grp):
                half = grp % 2
                pe.wait_ge(diag_done, h * GROUPS + (b * PH * GROUPS + grp + 1))
                for k in range(GROUP):
                    s = half * GROUP + k
                    for n in range(2):
                        mm = t.matmul(bank[2 * (b % 2) + n][:], diag[:, s, :], rows[s][:, D + n * 512:D + (n + 1) * 512],
                                      start=False, stop=False, skip_group_check=True)
                mm.then_inc(v_done, 1)

            pe.wait_ge(wq_in, 16)
            pe.wait_ge(keys_in, 16)
            transpose_x1(0)
            with pe.Fori(0, PH) as h:
                query(h, 0)
                query_T(h, 0)
                scores(h, 0)
            pe.wait_ge(filled, 1)
            for b in range(NB):
                if b >= 2:
                    pe.wait_ge(ffn_done, b - 1)
                for n in range(2):
                    mm = t.matmul(bank[2 * (b % 2) + n][:], zeros[:, 0:P], zeros, start=True, stop=False, skip_group_check=True)
                    if b == 0:
                        mm.then_inc(v_done, 1)
                if b < NB - 1:
                    transpose_x1(b + 1)
                with pe.Fori(0, PH) as h:
                    u0 = (b + 1) * PH
                    route = b < NB - 1
                    if route:
                        query(h, u0)
                    values(h, b, 0)
                    if route:
                        query_T(h, u0)
                    values(h, b, 1)
                    if route:
                        scores(h, u0)
                    values(h, b, 2)
                    values(h, b, 3)

        @block.scalar
        def _(act):
            a = nc.scalar
            st = Steps(act, act_steps)
            for i, (_, side, _, dst, scale) in enumerate(tiles):
                if i % 2 == 0:
                    act.wait_ge(proj_tile, i + 1)
                    src = bank[i % 8][0:RANK, :] if side == "a" else bank[i % 8][:]
                    a.activation(dst, src, ACT.Copy, scale=scale).then_inc(ev_act, 1)
            for hp in range(2):
                act.wait_ge(u_ready, hp + 1)
                a.activation(t1[:, hp, :], bank[hp][:], ACT.Abs, bias=bg_sb[:, hp:hp + 1]).then_inc(uabs, 1)
            act.wait_ge(uabs, 2)
            st(a.activation(t1, t1, ACT.Exp, scale=-1.0))
            st.wait()
            a.activation(t1, t1, ACT.Ln, bias=1.0).then_inc(uexp, 1)
            act.wait_ge(cumd, 2)
            a.activation(ecum, cum, ACT.Exp, scale=1.0 / GATE_TEMP).then_inc(ecumd, 1)
            a.activation(t1, cum, ACT.Exp, scale=-1.0 / GATE_TEMP).then_inc(ecumd, 1)
            act.wait_ge(dlast, 1)
            a.activation(t2, t2, ACT.Exp, scale=1.0 / GATE_TEMP).then_inc(kst_exp, 1)
            for i in range(2):
                act.wait_ge(kst_T, i + 1)
                a.activation(kstT[:, 2 * i:2 * i + 2], bank[2 + i][:].rearrange("p (b h n) -> p b h n", b=2, h=2),
                             ACT.Copy).then_inc(kst_copied, 1)
            act.wait_ge(st_ready, 7)
            for b in range(NB):
                for par in range(2):
                    for c in range(b, -1, -1):
                        n = zi(b, par, c)
                        act.wait_ge(z_ready, n + 1)
                        if par or b:
                            act.wait_ge(sp_ready, zi(b, par, b))
                        st(a.activation(lse[:, c, :], bank[n % ZB][:], ACT.Abs))
                        st.wait()
                        st(a.activation(lse[:, c, :], lse[:, c, :], ACT.Exp, scale=-1.0))
                        st.wait()
                        a.activation(lse[:, c, :], lse[:, c, :], ACT.Ln, bias=1.0).then_inc(l_ready, 1)
                    if b:
                        act.wait_ge(av_ready, b)
                    for c in range(b, -1, -1):
                        n = zi(b, par, c)
                        if c == b:
                            act.wait_ge(zmin_ready, 2 * b + par + 1)
                            a.activation(wT[:, par, c, :], zmin, ACT.Exp).then_inc(w_exp, 1)
                        else:
                            act.wait_ge(zc_ready, n + 1)
                            a.activation(wT[:, par, c, :], bank[n % ZB][:], ACT.Exp).then_inc(w_exp, 1)
                act.wait_ge(av_ready, b + 1)
                if b:
                    act.wait_ge(oT_ready, 2 * b)
                a.activation(o_n[:, 512:1024], bank[4][:], ACT.Copy).then_inc(o_copied, 1)
                act.wait_ge(go_ready, b + 1)
                o_v = o_n[:, 0:512].rearrange("p (h r n) -> p h r n", h=2, r=2)
                for par in range(2):
                    a.activation(o_v[:, :, par, :], bank[7 if par == 0 else 5][:, 0:256].rearrange("p (h n) -> p h n", h=2),
                                 ACT.Copy).then_inc(o_copied, 1)
                if b:
                    act.wait_ge(x1_ready, b)
                a.activation(egate, gg[:, b, :], ACT.Exp, scale=-1.0).then_inc(eg_ready, 1)
                act.wait_ge(ms_ready, b + 1)
                st(a.activation(ms[:], ms[:], ACT.Ln))
                st.wait()
                a.activation(ms[:], ms[:], ACT.Exp, scale=-0.5).then_inc(rs_ready, 1)
                for i in range(2):
                    act.wait_ge(oT_ready, 2 * b + i + 1)
                    a.activation(oT[:, 4 * i:4 * i + 4, :], bank[6 + i][:].rearrange("p (k n) -> p k n", k=4),
                                 ACT.Copy).then_inc(oT_copied, 1)
                act.wait_ge(var1, b + 1)
                st(a.activation(rstd[:], rstd[:], ACT.Ln))
                st.wait()
                a.activation(rstd[:], rstd[:], ACT.Exp, scale=-0.5).then_inc(rstd1, 1)

            def copy_x1T(b):
                act.wait_ge(x1T_done, b + 1)
                st(a.activation(x1T[:, 0:4, :], bank[6][:].rearrange("p (k n) -> p k n", k=4), ACT.Copy))
                st(a.activation(x1T[:, 4:8, :], bank[7][:].rearrange("p (k n) -> p k n", k=4), ACT.Copy))
                st.wait()
                act.sem_inc(x1T_copied, 1)

            def copy_q(h, u0):
                act.wait_ge(q_done, h + (u0 + 1))
                a.activation(q_sb, bank[4][:, 0:QW], ACT.Copy).then_inc(q_copied, 1)

            def copy_qT(h, u0):
                act.wait_ge(qT_done, h + (u0 + 1))
                a.activation(qT_sb, bank[5][:, 0:QW].rearrange("p (s n) -> p s n", s=2), ACT.Copy).then_inc(qT_copied, 1)

            def gate_exp(h, u0):
                act.wait_ge(best_ready, h + (u0 + 1))
                a.activation(eb, best, ACT.Exp, bias=nbest, accum_out=esum).then_inc(gexp, 1)

            def gelu(h, b, grp):
                act.wait_ge(dot_done, h * GROUPS + (b * PH * GROUPS + grp + 1))
                a.activation(acts[:, grp % 2, :], dots[:, grp % 2, :], ACT.Gelu).then_inc(gelu_done, 1)

            def diagonals(h, b, grp):
                act.wait_ge(w_done, h * GROUPS + (b * PH * GROUPS + grp + 2))
                act.wait_ge(v_done, h * GROUPS + (b * PH * GROUPS + grp + 1))
                for k in range(GROUP):
                    s = (grp % 2) * GROUP + k
                    ins = a.activation(diag[:, s, :], ident[:], ACT.Copy, scale=wts[:, grp % 2, k:k + 1])
                ins.then_inc(diag_done, 1)

            copy_x1T(0)
            with act.Fori(0, PH) as h:
                copy_q(h, 0)
                copy_qT(h, 0)
                gate_exp(h, 0)
            for b in range(NB):
                route = b < NB - 1
                if route:
                    copy_x1T(b + 1)
                with act.Fori(0, PH) as h:
                    u0 = (b + 1) * PH
                    gelu(h, b, 0)
                    diagonals(h, b, 0)
                    if route:
                        copy_q(h, u0)
                    gelu(h, b, 1)
                    diagonals(h, b, 1)
                    if route:
                        copy_qT(h, u0)
                    gelu(h, b, 2)
                    diagonals(h, b, 2)
                    gelu(h, b, 3)
                    diagonals(h, b, 3)
                    if route:
                        gate_exp(h, u0)
                act.wait_ge(var2, b + 1)
                st(a.activation(rstd[:], rstd[:], ACT.Ln))
                st.wait()
                a.activation(rstd[:], rstd[:], ACT.Exp, scale=-0.5).then_inc(rstd2, 1)

        @block.vector
        def _(dve):
            v = nc.vector
            st = Steps(dve, dve_steps)
            for i, (_, side, _, dst, scale) in enumerate(tiles):
                if i % 2 == 1:
                    dve.wait_ge(proj_tile, i + 1)
                    src = bank[i % 8][0:RANK, :] if side == "a" else bank[i % 8][:]
                    v.tensor_scalar(dst, src, scale, None, ALU.mult).then_inc(ev_dve, 1)
            for hp in range(2):
                dve.wait_ge(uabs, hp + 1)
                st(v.tensor_scalar(t2[:, hp, :], bank[hp][:], bg_sb[:, hp:hp + 1], 0.0, ALU.add, ALU.min))
            st.wait()
            dve.wait_ge(uexp, 1)
            st(v.tensor_tensor(t2, t2, t1, ALU.subtract))
            st.wait()
            dve.wait_ge(made, 1)
            for hp in range(2):
                v.tensor_tensor_scan(cum[:, hp, :], carry[:], t2[:, hp, :], 0.0, ALU.mult, ALU.add).then_inc(cumd, 1)
            dve.wait_ge(cumd, 2)
            for hp in range(2):
                c_v = cum[:, hp, :].rearrange("p (c t) -> p c t", t=GC)
                ins = v.tensor_tensor(t2[:, hp, :].rearrange("p (c t) -> p c t", t=GC),
                                      c_v[:, :, GC - 1:GC].to_broadcast([P, SEQ // GC, GC]), c_v, ALU.subtract)
            ins.then_inc(dlast, 1)
            dve.wait_ge(ecumd, 2)
            dve.wait_ge(ev_act, (NT + 1) // 2)
            st(v.tensor_tensor(kin, kgT, t1, ALU.mult))
            st(v.scalar_tensor_tensor(out=qgT, in0=qgT, scalar=GDK ** -0.5, in1=ecum, op0=ALU.mult, op1=ALU.mult))
            dve.wait_ge(kst_exp, 1)
            st.wait()
            v.tensor_tensor(kgT, kgT, t2, ALU.mult).then_inc(qk_ready, 1)
            for c in range(7):
                dve.wait_ge(su_ready, c + 1)
                for hp in range(2):
                    su = bank[4 + c % 4][:, hp * GDV:(hp + 1) * GDV]
                    if c == 0:
                        ins = v.tensor_copy(state[:, 1, hp, :], su)
                    else:
                        if hp == 0:
                            dve.wait_ge(st_ready, c)
                        ins = v.scalar_tensor_tensor(out=state[:, c + 1, hp, :], in0=state[:, c, hp, :],
                                                     scalar=ecum[:, hp, (c + 1) * GC - 1:(c + 1) * GC], in1=su,
                                                     op0=ALU.mult, op1=ALU.add)
                ins.then_inc(st_ready, 1)

            def layer_norm(y, b, g_row, var_sem, rstd_sem, dst, done):
                for n in range(2):
                    st(v.bn_stats(stats[:, n, :], y[:, n * 512:(n + 1) * 512]))
                st.wait()
                st(v.bn_aggr(mv[:], stats[:]))
                st.wait()
                v.tensor_scalar(rstd[:], mv[:, 1:2], EPS, None, ALU.add).then_inc(var_sem, 1)
                dve.wait_ge(rstd_sem, b + 1)
                st(v.tensor_scalar(y, y, mv[:, 0:1], rstd[:], ALU.subtract, ALU.mult))
                st.wait()
                st(v.tensor_tensor(y, y, ln_sb[:, g_row, :], ALU.mult))
                st.wait()
                v.tensor_tensor(dst, y, ln_sb[:, g_row + 1, :], ALU.add).then_inc(done, 1)

            for b in range(NB):
                for par in range(2):
                    for c in range(b, -1, -1):
                        n = zi(b, par, c)
                        dve.wait_ge(l_ready, n + 1)
                        if b:
                            dve.wait_ge(zc_ready, zi(b, 0, b))
                        if c == b:
                            st(v.scalar_tensor_tensor(out=sp[:, par, c, :], in0=bank[n % ZB][:], scalar=0.0,
                                                      in1=lse[:, c, :], op0=ALU.max, op1=ALU.add))
                            st.wait()
                            s_v = sp[:, par, c, :].rearrange("p (j q) -> p j q", j=4)
                            v.tensor_tensor(s_v, s_v, before[:, None, :].to_broadcast([P, 4, P]), ALU.mult).then_inc(sp_ready, 1)
                        else:
                            v.scalar_tensor_tensor(out=sp[:, par, c, :], in0=bank[n % ZB][:], scalar=0.0,
                                                   in1=lse[:, c, :], op0=ALU.max, op1=ALU.add).then_inc(sp_ready, 1)
                    n = zi(b, par, b)
                    dve.wait_ge(zc_ready, n + 1)
                    if n:
                        dve.wait_ge(w_exp, n)
                    v.tensor_scalar(zmin, bank[n % ZB][:], 0.0, None, ALU.min).then_inc(zmin_ready, 1)
                    dve.wait_ge(w_exp, n + 1)
                    w_v = wT[:, par, b, :].rearrange("p (j q) -> p j q", j=4)
                    v.tensor_tensor(w_v, w_v, before[:, None, :].to_broadcast([P, 4, P]), ALU.mult).then_inc(w_masked, 1)
                dve.wait_ge(att_ready, b + 1)
                if b:
                    dve.wait_ge(go_ready, b)
                for par in range(2):
                    ins = v.tensor_tensor(attm[:, par], bank[5 + par][:, 0:256].rearrange("p (h t) -> p h t", h=2),
                                          chunk_mask[:, None, :].to_broadcast([P, 2, P]), ALU.mult)
                ins.then_inc(attm_ready, 1)
                dve.wait_ge(o_copied, 3 * (b + 1))
                st(v.tensor_tensor(sq, o_n, o_n, ALU.mult))
                st.wait()
                st(v.tensor_reduce(ms[:, 0:GH], sq[:, 0:512].rearrange("p (h n) -> p h n", h=GH), AX_X, ALU.add))
                st(v.tensor_reduce(ms[:, GH:], sq[:, 512:].rearrange("p (h n) -> p h n", h=SH), AX_X, ALU.add))
                st.wait()
                st(v.tensor_scalar(ms[:, 0:GH], ms[:, 0:GH], 1.0 / GDV, EPS, ALU.mult, ALU.add))
                st(v.tensor_scalar(ms[:, GH:], ms[:, GH:], 1.0 / SD, EPS, ALU.mult, ALU.add))
                st.wait()
                dve.sem_inc(ms_ready, 1)
                dve.wait_ge(eg_ready, b + 1)
                st(v.tensor_scalar(egate, egate, 1.0, None, ALU.add))
                st.wait()
                st(v.reciprocal(egate, egate))
                st.wait()
                st(v.tensor_tensor(egate, egate, gg[:, b, :], ALU.mult))
                dve.wait_ge(rs_ready, b + 1)
                og = o_n[:, 0:512].rearrange("p (h n) -> p h n", h=GH)
                os_ = o_n[:, 512:1024].rearrange("p (h n) -> p h n", h=SH)
                st(v.tensor_tensor(og, og, ms[:, 0:GH, None].to_broadcast([P, GH, GDV]), ALU.mult))
                st(v.tensor_tensor(os_, os_, ms[:, GH:, None].to_broadcast([P, SH, SD]), ALU.mult))
                st.wait()
                if b == 0:
                    dve.wait_ge(consts_in, 80)
                    dve.wait_ge(x_in, 16)
                st(v.tensor_tensor(o_n, o_n, gains_sb[:], ALU.mult))
                st.wait()
                v.tensor_tensor(o_n[:, 0:512], o_n[:, 0:512], egate, ALU.mult).then_inc(on_ready, 1)
                dve.wait_ge(mix_ready, b + 1)
                for n in range(2):
                    xs = x_sb[:, b, n * 512:(n + 1) * 512]
                    st(v.scalar_tensor_tensor(out=xs, in0=xs, scalar=ALPHA, in1=bank[4 + n][:], op0=ALU.mult, op1=ALU.add))
                st.wait()
                layer_norm(x_sb[:, b, :], b, 0, var1, rstd1, x_sb[:, b, :], x1_ready)

            v.memset(zeros, 0.0).then_inc(filled, 1)
            dve.sem_inc(sc_copied, 1)
            dve.sem_inc(w_done, 1)

            def copy_scores(h, u0):
                dve.wait_ge(sc_done, h + (u0 + 1))
                st(v.tensor_copy(sc, bank[6][:, 0:QW].rearrange("p (s n) -> p s n", s=2)))
                st.wait()
                dve.sem_inc(sc_copied, 1)

            def top16(src, src2, vals, where):
                st.wait()
                st(v.max(vals[:, 0:8], src))
                st.wait()
                st(v.max_index(where[:, 0:8], vals[:, 0:8], src))
                st(v.match_replace(src2, vals[:, 0:8], src, LOWEST))
                st.wait()
                st(v.max(vals[:, 8:16], src2))
                st.wait()
                st(v.max_index(where[:, 8:16], vals[:, 8:16], src2))

            def candidates(h, u0):
                st.wait()
                st(v.tensor_tensor(cand.rearrange("p (i j) -> p i j", i=TOPK),
                                   top[:, 0, :, None].to_broadcast([P, TOPK, TOPK]),
                                   top[:, 1, None, :].to_broadcast([P, TOPK, TOPK]), ALU.add))
                top16(cand, cand2, best, pos[:, 0, :])
                st.wait()
                v.tensor_scalar(nbest, best[:, 0:1], -1.0, None, ALU.mult).then_inc(best_ready, 1)

            def finish_route(h, b, u0):
                par = (b % 2) * SLOTS
                st(v.tensor_scalar(pos[:, 1, :], pos[:, 0, :], TOPK - 1, None, ALU.bitwise_and))
                st(v.tensor_copy(topf, topi[:]))
                st.wait()
                st(v.tensor_scalar(pos[:, 0, :], pos[:, 0, :], 4, None, ALU.logical_shift_right))
                st.wait()
                st(v.tensor_copy(posf, pos[:]))
                st.wait()
                for s in range(2):
                    st(v.tensor_tensor(onehot[:, s], posf[:, s, :, None].to_broadcast([P, TOPK, TOPK]),
                                       iota16[:, None, :].to_broadcast([P, TOPK, TOPK]), ALU.is_equal))
                st.wait()
                for s in range(2):
                    st(v.tensor_tensor(onehot[:, s], onehot[:, s], topf[:, s, None, :].to_broadcast([P, TOPK, TOPK]), ALU.mult))
                st.wait()
                st(v.tensor_reduce(sel, onehot, AX_X, ALU.add))
                st.wait()
                st(v.scalar_tensor_tensor(out=idx[:, bass.ds(h * TOPK + par, TOPK)], in0=sel[:, 0, :], scalar=float(NKEYS),
                                          in1=sel[:, 1, :], op0=ALU.mult, op1=ALU.add))
                dve.wait_ge(gexp, h + (u0 + 1))
                st(v.reciprocal(esum, esum))
                st.wait()
                st(v.tensor_scalar(gates[:, bass.ds(h * TOPK + par, TOPK)], eb, esum, None, ALU.mult))
                st.wait()
                dve.sem_inc(routed, 1)

            def dot(h, b, grp):
                half = grp % 2
                for k in range(GROUP):
                    s = half * GROUP + k
                    dve.wait_ge(landed[s], h * (16 * GROUPS // 2) + (16 * (b * PH * GROUPS // 2 + grp // 2 + 1)))
                    u = rows[s][:, 0:D]
                    ins = v.tensor_tensor_reduce(u, u, x_sb[:, b, :], 1.0, 0.0, ALU.mult, ALU.add, dots[:, half, k:k + 1])
                ins.then_inc(dot_done, 1)

            def weigh(h, b, grp):
                half = grp % 2
                dve.wait_ge(gelu_done, h * GROUPS + (b * PH * GROUPS + grp + 1))
                v.tensor_tensor(wts[:, half, :], acts[:, half, :], gate_now[:, grp * GROUP:(grp + 1) * GROUP],
                                ALU.mult).then_inc(w_done, 1)

            st.restart()
            with dve.Fori(0, PH) as h:
                copy_scores(h, 0)
                top16(sc[:, 0, :], sc2[:, 0, :], top[:, 0, :], topi[:, 0, :])
                top16(sc[:, 1, :], sc2[:, 1, :], top[:, 1, :], topi[:, 1, :])
                candidates(h, 0)
                finish_route(h, 0, 0)
                st.restart()
            for b in range(NB):
                route = b < NB - 1
                u0 = (b + 1) * PH
                with dve.Fori(0, PH) as h:
                    dot(h, b, 0)
                    dve.wait_ge(w_done, h * GROUPS + (b * PH * GROUPS + 1))
                    st(v.tensor_copy(gate_now, gates[:, bass.ds(h * TOPK + (b % 2) * SLOTS, TOPK)]))
                    st.wait()
                    weigh(h, b, 0)
                    dot(h, b, 1)
                    weigh(h, b, 1)
                    dot(h, b, 2)
                    if route:
                        copy_scores(h, u0)
                        top16(sc[:, 0, :], sc2[:, 0, :], top[:, 0, :], topi[:, 0, :])
                    weigh(h, b, 2)
                    dot(h, b, 3)
                    if route:
                        top16(sc[:, 1, :], sc2[:, 1, :], top[:, 1, :], topi[:, 1, :])
                    weigh(h, b, 3)
                    if route:
                        candidates(h, u0)
                        finish_route(h, b + 1, u0)
                    st.restart()
                dve.wait_ge(v_done, 2 + (b + 1) * PH * GROUPS)
                if b:
                    dve.wait_ge(stored, 16 * b)
                for n in range(2):
                    st(v.scalar_tensor_tensor(out=y2[:, n * 512:(n + 1) * 512], in0=x_sb[:, b, n * 512:(n + 1) * 512],
                                              scalar=ALPHA, in1=bank[2 * (b % 2) + n][:], op0=ALU.mult, op1=ALU.add))
                st.wait()
                dve.sem_inc(ffn_done, 1)
                layer_norm(y2, b, 2, var2, rstd2, y2, y_ready)
                st.restart()


def kernel(**inputs):
    import numpy as _np
    import concourse.bacc as _bacc
    from concourse import mybir as _mybir
    from concourse.bass_utils import run_bass_kernel_spmd as _run

    i = {k: _np.asarray(v) for k, v in inputs.items()}
    x = i["x"].reshape(512, 1024)
    laid = {
        "x": x,
        "xT": x.T,
        "w_in": i["w_in"][0],
        "w_gate": i["w_gla_gate"][0],
        "b_gate": i["b_gla_gate"].reshape(2, 128).T,
        "gains": _np.concatenate([i["gla_norm_g"].reshape(512), i["sb_norm_g"].reshape(512)]),
        "w_out": i["w_out"][0],
        "ln": _np.stack([i[k].reshape(1024) for k in ("ln1_g", "ln1_b", "ln2_g", "ln2_b")]),
        "w_query": i["peer_w_query"][0],
        "keysT": i["peer_sub_keys"].reshape(16, 128, 128).transpose(2, 0, 1).reshape(128, 2048),
        "experts": _np.concatenate([i["peer_u"][0], i["peer_v"][0]], axis=1),
    }
    nc = _bacc.Bacc("TRN2", target_bir_lowering=False, num_devices=1)
    arrays, args = {}, []
    for name, a in laid.items():
        a = _np.ascontiguousarray(a)
        arrays[f"in_{name}_dram"] = a
        args.append(nc.dram_tensor(f"in_{name}_dram", a.shape, _mybir.dt.from_np(a.dtype), kind="ExternalInput").ap())
    args.append(nc.dram_tensor("out_0_dram", (512, 1024), _mybir.dt.float32, kind="ExternalOutput").ap())
    hybrid_layer(nc, *args)
    r = _run(nc, [arrays], core_ids=[0])
    return r.results[0]["out_0_dram"].reshape(1, 512, 1024)
```

```python
from contextlib import ExitStack

import concourse.bass as bass
from concourse import mybir

F32 = mybir.dt.float32
U32 = mybir.dt.uint32
ALU = mybir.AluOpType
ACT = mybir.ActivationFunctionType
AX_X = mybir.AxisListType.X

P = 128
D = 1024
SEQ = 512
NB = SEQ // P
KC = D // P
GH, GDK, GDV, GC = 4, 64, 128, 64
RANK = 16
GATE_TEMP = 16.0
SH, SD = 8, 64
PH, NKEYS, TOPK = 8, 128, 16
QW = 2 * P
SLOTS = PH * TOPK
ALPHA = 2.0 ** 0.25
EPS = 1e-5
LOWEST = -3.0e38

RING = 8
GROUP = 4
GROUPS = TOPK // GROUP
SP_BUFS, W_BUFS = 6, 8
ZB = 3
RATES = [(0, 1), (0, 1), (2, 1), (2, 1)]
SILU_AT = 14
PROJ_BANKS = 6
U_AT, KST_AT, SU_AT = 8, 12, 13

C_QK, C_VG, C_GG, C_A, C_QS, C_KS, C_VS = 0, 512, 1024, 1536, 1552, 2064, 2576
W_GROUPS = [C_QK, C_VG, C_GG, C_QS, C_KS, C_VS]
WBUFS = 3


class Steps:

    def __init__(self, eng, sem):
        self.eng, self.sem, self.n = eng, sem, 0

    def __call__(self, ins):
        self.n += 1
        ins.then_inc(self.sem, 1)

    def wait(self):
        self.eng.wait_ge(self.sem, self.n)

    def restart(self):
        if self.n:
            self.wait()
        self.eng.sem_clear(self.sem)
        self.n = 0


def hybrid_layer(nc, x, xT, w_in, w_gate, b_gate, gains, w_out, ln, w_query, keysT, experts, out):
    ctx = ExitStack()
    with ctx:
        def sb(name, shape, dt=F32):
            return ctx.enter_context(nc.sbuf_tensor(name, shape, dt))

        def sem(name):
            return ctx.enter_context(nc.semaphore(name))

        bank = [ctx.enter_context(nc.psum_tensor(f"bank{i}", [P, 512], F32)) for i in range(8)]

        x_sb = sb("x_sb", [P, NB, D])
        x1T = sb("x1T", [P, KC, P])
        ln_sb = sb("ln_sb", [P, 2, D])
        rt = sb("rt", [P, 2048])
        small = sb("small", [P, 480])
        gains_sb = sb("gains_sb", [P, D])
        ring = sb("ring", [P, RING * 2 * D])
        big = sb("big", [P, KC * PH * QW])
        keys = sb("keys", [P, 2 * PH * NKEYS])
        scr = sb("scr", [P, 6144])
        ident = sb("ident", [P, P])
        neg_tri = sb("neg_tri", [P, P])
        neg_one = sb("neg_one", [P, P])
        before = sb("before", [P, P])
        chunk_mask = sb("chunk_mask", [P, P])
        iota16 = sb("iota16", [P, TOPK])
        bg_sb = sb("bg_sb", [P, 2])
        stats = sb("stats", [P, 2, 6])
        mv = sb("mv", [P, 2])
        rstd = sb("rstd", [P, 1])
        ms = sb("ms", [P, GH + SH])

        xT_sb = ring[:, 0:KC * SEQ].rearrange("p (k t) -> p k t", k=KC)
        w_buf = [ring[:, (i + 1) * 4096:(i + 2) * 4096].rearrange("p (k n) -> p k n", k=KC)
                 for i in range(WBUFS)]
        wa_sb = scr[:, 4096:4096 + KC * RANK].rearrange("p (k n) -> p k n", k=KC)
        wg_sb = scr[0:RANK, 4096 + KC * RANK:4096 + KC * RANK + 256]
        qgT = big[:, 0:1024].rearrange("p (h t) -> p h t", h=2)
        kgT = big[:, 1024:2048].rearrange("p (h t) -> p h t", h=2)
        qsT = big[:, 2048:4096].rearrange("p (h t) -> p h t", h=4)
        ksT = big[:, 4096:6144].rearrange("p (h t) -> p h t", h=4)
        vg = big[:, 6144:8192].rearrange("p (b n) -> p b n", b=NB)
        gg = big[:, 8192:10240].rearrange("p (b n) -> p b n", b=NB)
        vs = big[:, 10240:12288].rearrange("p (b n) -> p b n", b=NB)
        aT = big[0:RANK, 12288:12800]
        kin = big[:, 12800:13824].rearrange("p (h t) -> p h t", h=2)
        oT = big[:, 13824:14848].rearrange("p (k t) -> p k t", k=KC)
        attm = big[:, 14848:15360].rearrange("p (r h t) -> p r h t", r=2, h=2)
        carry = big[:, 15360:15872]
        wo_sb = ring[:, 0:8192].rearrange("p (k n) -> p k n", k=KC)
        wT = ring[:, 8192:12288].rearrange("p (c n) -> p c n", c=W_BUFS)
        wq_buf = [ring[:, 12288 + i * 2048:14336 + i * 2048].rearrange("p (k n) -> p k n", k=KC) for i in range(2)]
        o_n = big[:, 1024:2048]
        sig = rt[:, 1024:2048].rearrange("p (j n) -> p j n", j=2)
        kstT = rt[:, 0:1024].rearrange("p (b h n) -> p b h n", b=NB, h=2)
        cum = scr[:, 0:1024].rearrange("p (h t) -> p h t", h=2)
        ecum = scr[:, 1024:2048].rearrange("p (h t) -> p h t", h=2)
        t1 = scr[:, 2048:3072].rearrange("p (h t) -> p h t", h=2)
        t2 = scr[:, 3072:4096].rearrange("p (h t) -> p h t", h=2)
        state = scr[:, 4096:6144].rearrange("p (c h n) -> p c h n", c=8, h=2)
        sp = scr[:, 0:3072].rearrange("p (c n) -> p c n", c=SP_BUFS)
        zmin = scr[:, 3072:3584]
        sq = big[:, 15360:16384]
        wq_sb = big[:, :].rearrange("p (k n) -> p k n", k=KC)
        rows = [ring[:, i * 2 * D:(i + 1) * 2 * D] for i in range(RING)]
        q_sb = rt[:, 0:256]
        qT_sb = rt[:, 256:512].rearrange("p (s t) -> p s t", s=2)
        sc = rt[:, 512:768].rearrange("p (s n) -> p s n", s=2)
        sc2 = rt[:, 768:1024].rearrange("p (s n) -> p s n", s=2)
        cand = rt[:, 1024:1280]
        cand2 = rt[:, 1280:1536]
        onehot = rt[:, 1536:2048].rearrange("p (s k a) -> p s k a", s=2, k=TOPK)
        gates = small[:, 0:256]
        top = small[:, 256:288].rearrange("p (s k) -> p s k", s=2)
        topf = small[:, 288:320].rearrange("p (s k) -> p s k", s=2)
        posf = small[:, 320:352].rearrange("p (s k) -> p s k", s=2)
        sel = small[:, 352:384].rearrange("p (s k) -> p s k", s=2)
        best = small[:, 384:400]
        eb = small[:, 400:416]
        nbest = small[:, 416:417]
        esum = small[:, 417:418]
        gate_now = small[:, 424:440]
        dots = small[:, 440:448].rearrange("p (s k) -> p s k", s=2)
        acts = small[:, 448:456].rearrange("p (s k) -> p s k", s=2)
        wts = small[:, 456:464].rearrange("p (s k) -> p s k", s=2)
        diag = scr[:, 0:1024].rearrange("p (s n) -> p s n", s=RING)
        y2 = scr[:, 1024:2048]
        zeros = scr[:, 2048:2560]
        topi = sb("topi", [P, 2, TOPK], U32)
        pos = sb("pos", [P, 2, TOPK], U32)
        idx = sb("idx", [P, 2 * SLOTS], U32)
        idx_now = sb("idx_now", [P, 2, GROUP], U32)

        xT_in, wa_in, x_in, consts_in, wo_in, wq_in, keys_in, ln2_in = (
            sem(n) for n in ("xT_in", "wa_in", "x_in", "consts_in", "wo_in", "wq_in", "keys_in", "ln2_in"))
        wq_head_in = [sem(f"wq_head_in{i}") for i in range(2)]
        sig_log, sig_sum, sig_exp, silu_done = (sem(n) for n in ("sig_log", "sig_sum", "sig_exp", "silu_done"))
        mix_part, mix_used = sem("mix_part"), sem("mix_used")
        w_in_sem = [sem(f"w_in{i}") for i in range(WBUFS)]
        made, filled = sem("made"), sem("filled")
        proj_tile, ev_act, ev_dve = (sem(n) for n in ("proj_tile", "ev_act", "ev_dve"))
        act_steps, dve_steps, pool_steps = (sem(n) for n in ("act_steps", "dve_steps", "pool_steps"))
        u_ready, uabs, umin, uexp, cumd, ecumd, kst_exp, dlast, qk_ready, kst_T, kst_copied, su_ready, st_ready = (
            sem(n) for n in ("u_ready", "uabs", "umin", "uexp", "cumd", "ecumd", "kst_exp", "dlast", "qk_ready",
                             "kst_T", "kst_copied", "su_ready", "st_ready"))
        z_ready, l_ready, sp_ready, zc_ready, zmin_ready, w_exp, w_masked, att_ready, attm_ready, av_ready, go_ready = (
            sem(n) for n in ("z_ready", "l_ready", "sp_ready", "zc_ready", "zmin_ready", "w_exp", "w_masked",
                             "att_ready", "attm_ready", "av_ready", "go_ready"))
        o_copied, ms_ready, rs_ready, on_ready, oT_ready, oT_copied, var1, rstd1, x1_ready = (
            sem(n) for n in ("o_copied", "ms_ready", "rs_ready", "on_ready", "oT_ready", "oT_copied",
                             "var1", "rstd1", "x1_ready"))
        x1T_done, x1T_copied, q_done, q_copied, qT_done, qT_copied, sc_done, sc_copied, best_ready, gexp, routed = (
            sem(n) for n in ("x1T_done", "x1T_copied", "q_done", "q_copied", "qT_done", "qT_copied", "sc_done",
                             "sc_copied", "best_ready", "gexp", "routed"))
        landed = [sem(f"landed{i}") for i in range(RING)]
        dot_done, gelu_done, w_done, diag_done, v_done, ffn_done, var2, rstd2, y_ready, stored = (
            sem(n) for n in ("dot_done", "gelu_done", "w_done", "diag_done", "v_done", "ffn_done", "var2", "rstd2",
                             "y_ready", "stored"))

        tiles = []
        for g, c in enumerate(W_GROUPS):
            for j in range(4):
                if c == C_QK:
                    tiles.append((g, "w", j, (qgT, kgT)[j // 2][:, j % 2, :], 1.0))
                elif c == C_QS:
                    tiles.append((g, "w", j, qsT[:, j, :], SD ** -0.5))
                elif c == C_KS:
                    tiles.append((g, "w", j, ksT[:, j, :], 1.0))
                else:
                    tiles.append((g, "x", j, {C_VG: vg, C_GG: gg, C_VS: vs}[c][:, j, :], 1.0))
            if g == 0:
                tiles.append((0, "a", 0, aT, 1.0))
        NT = len(tiles)
        group_end = [max(i for i, tile in enumerate(tiles) if tile[0] == g) + 1 for g in range(len(W_GROUPS))]

        block = ctx.enter_context(nc.Block())

        sb_tiles = [(b, par, c) for b in range(NB) for par in range(2) for c in range(b, -1, -1)]
        NZ = len(sb_tiles)
        first = {}
        for n, (b, par, c) in enumerate(sb_tiles):
            first.setdefault((b, par), n)
        last = {(b, par): first[b, par] + b for b, par in first}

        def tail(b):
            return ([("heads_out", b), ("copy_heads", b), ("att", b + 1), ("head_squares", b), ("mask_att", b + 1),
                     ("head_roots", b), ("gate_heads", b),
                     ("turn", (b, 0)), ("copy_oT", (b, 0)), ("turn", (b, 1)), ("copy_oT", (b, 1)),
                     ("mix", (b, 0)), ("residual", (b, 0)), ("mix", (b, 1)), ("residual", (b, 1)),
                     ("variance", b), ("root", b), ("normalise", b)])

        def routing(h):
            make = [("query", h), ("copy_q", h), ("query_T", h), ("copy_qT", h), ("scores", h), ("copy_scores", h)]
            choose = [("top_a", h - 1), ("top_b", h - 1), ("best", h - 1), ("gate_exp", h - 1), ("routed", h - 1)]
            order = []
            for i in range(6):
                order += make[i:i + 1] * (h < PH) + choose[i:i + 1] * (h > 0)
            return order

        plan = [("z", 0), ("att", 0), ("mask_att", 0), ("z", 1), ("sp", 0)]
        tails, routes = [], []

        def deal(n_tail, n_route):
            for _ in range(max(n_tail, n_route)):
                if n_tail > 0 and tails:
                    plan.append(tails.pop(0))
                    n_tail -= 1
                    if plan[-1] == ("normalise", 0):
                        routes.extend([("turn_x1", 0), ("copy_x1T", 0), ("turn_x1", 1), ("copy_x1T", 1)])
                        for h in range(PH + 1):
                            routes.extend(routing(h))
                if n_route > 0 and routes:
                    plan.append(routes.pop(0))
                    n_route -= 1

        for n, (b, par, c) in enumerate(sb_tiles):
            rt_, tt_ = RATES[b]
            if n + 2 < NZ:
                plan.append(("z", n + 2))
            deal(tt_, rt_)
            if n + 1 < NZ:
                plan.append(("sp", n + 1))
            deal(tt_, rt_)
            plan.append(("tail_sums", n))
            if n == first[b, par] and (b or par):
                if par:
                    plan.append(("values_out", b))
                else:
                    plan.append(("heads_out", b - 1))
                    tails.extend(tail(b - 1)[1:])
            deal(tt_, rt_)
            plan.append(("w", n))
            deal(tt_, rt_)
        plan.append(("heads_out", NB - 1))
        tails.extend(step for step in tail(NB - 1)[1:] if step[1] != NB)
        while tails or routes:
            deal(1, 2)

        units = lambda b, h: b * PH + h

        @block.sync
        def _(sp_eng):
            xT_v = xT.rearrange("(k p) t -> p k t", p=P)
            w_v = w_in.rearrange("(k p) n -> p k n", p=P)
            sp_eng.dma_start(xT_sb, xT_v).then_inc(xT_in, 16)
            for g, c in enumerate(W_GROUPS):
                if g >= WBUFS:
                    sp_eng.wait_ge(proj_tile, group_end[g - WBUFS])
                sp_eng.dma_start(w_buf[g % WBUFS], w_v[:, :, c:c + 512]).then_inc(w_in_sem[g % WBUFS], 16)
                if g == 0:
                    with nc.allow_non_contiguous_dma(reason="16 columns"):
                        sp_eng.dma_start(wa_sb, w_v[:, :, C_A:C_A + RANK]).then_inc(wa_in, 16)
                    sp_eng.dma_start(wg_sb, w_gate).then_inc(wa_in, 16)
                    sp_eng.dma_start(bg_sb[:], b_gate).then_inc(wa_in, 16)
            sp_eng.dma_start(x_sb[:], x.rearrange("(b p) d -> p b d", p=P)).then_inc(x_in, 16)
            sp_eng.dma_start(gains_sb[:], gains.partition_broadcast(P)).then_inc(consts_in, 16)
            for i in range(2):
                sp_eng.dma_start(ln_sb[:, i, :], ln[i:i + 1, :].rearrange("a d -> (a d)").partition_broadcast(P)).then_inc(consts_in, 16)
            sp_eng.wait_ge(proj_tile, NT)
            sp_eng.dma_start(wo_sb, w_out.rearrange("(k p) n -> p k n", p=P)).then_inc(wo_in, 16)
            wq_v = w_query.rearrange("(k p) n -> p k n", p=P)
            sp_eng.dma_start(keys[:], keysT).then_inc(keys_in, 16)
            for h in range(PH):
                if h >= 2:
                    sp_eng.wait_ge(q_done, h - 1)
                sp_eng.dma_start(wq_buf[h % 2], wq_v[:, :, h * QW:(h + 1) * QW]).then_inc(wq_head_in[h % 2], 16)
            sp_eng.wait_ge(mix_part, 2 * NB)
            sp_eng.dma_start(wq_sb, wq_v).then_inc(wq_in, 16)
            sp_eng.wait_ge(x1_ready, NB)
            for i in range(2):
                sp_eng.dma_start(ln_sb[:, i, :], ln[2 + i:3 + i, :].rearrange("a d -> (a d)").partition_broadcast(P)).then_inc(ln2_in, 16)
            out_v = out.rearrange("(b p) d -> b p d", p=P)
            for b in range(NB):
                sp_eng.wait_ge(y_ready, b + 1)
                sp_eng.dma_start(out_v[b], y2).then_inc(stored, 16)
            sp_eng.wait_ge(stored, 16 * NB)

        @block.gpsimd
        def _(pool):
            g = nc.gpsimd
            st = Steps(pool, pool_steps)
            g.memset(ident[:], 0.0)
            g.memset(neg_one[:], -1.0)
            g.memset(neg_tri[:], -1.0)
            g.memset(before[:], 1.0)
            g.memset(chunk_mask[:], 1.0)
            g.memset(carry, 1.0)
            st(g.iota(iota16[:], [[1, TOPK]], base=0, channel_multiplier=0, allow_small_or_imprecise_dtypes=True))
            st.wait()
            g.affine_select(out=ident[:], in_=ident[:], compare_op=ALU.not_equal, fill=1.0, base=0,
                            pattern=[[-1, P]], channel_multiplier=1)
            g.affine_select(out=neg_tri[:], in_=neg_tri[:], compare_op=ALU.is_ge, fill=0.0, base=0,
                            pattern=[[-1, P]], channel_multiplier=1)
            g.affine_select(out=before[:], in_=before[:], compare_op=ALU.is_gt, fill=0.0, base=0,
                            pattern=[[1, P]], channel_multiplier=-1)
            g.memset(carry.rearrange("p (c t) -> p c t", t=GC)[:, :, 0:1], 0.0)
            st(g.affine_select(out=chunk_mask[:], in_=chunk_mask[:], compare_op=ALU.is_ge, fill=0.0, base=0,
                               pattern=[[1, P]], channel_multiplier=-1))
            st.wait()
            g.affine_select(out=chunk_mask[:, GC:P], in_=chunk_mask[:, GC:P], compare_op=ALU.is_ge, fill=0.0, base=-GC,
                            pattern=[[0, GC]], channel_multiplier=1).then_inc(made, 1)
            for n, (b, _, c) in enumerate(sb_tiles):
                if c == b:
                    pool.wait_ge(w_exp, n + 1)
                    w_v = wT[:, n % W_BUFS, :].rearrange("p (j q) -> p j q", j=4)
                    g.tensor_tensor(w_v, w_v, before[:, None, :].to_broadcast([P, 4, P]), ALU.mult).then_inc(w_masked, 1)
            pool.wait_ge(mix_part, 2 * NB)
            for b in range(NB):
                st.restart()
                with pool.Fori(0, PH) as h:
                    for grp in range(GROUPS):
                        half = grp % 2
                        if grp == 0:
                            pool.wait_ge(routed, h + (b * PH + 1))
                        for k in range(GROUP):
                            s = half * GROUP + k
                            i = grp * GROUP + k
                            pool.wait_ge(v_done, h * TOPK + (b * SLOTS + i + 1))
                            st(g.tensor_copy(idx_now[:, half, k:k + 1], idx[:, bass.ds(h * TOPK + ((b % 2) * SLOTS + i), 1)]))
                            st.wait()
                            g.indirect_dma_start(rows[s], None, experts, bass.IndirectOffsetOnAxis(
                                ap=idx_now[:, half, k:k + 1], axis=0)).then_inc(landed[s], 16)
                    st.restart()

        @block.tensor
        def _(pe):
            t = nc.tensor
            pe.wait_ge(xT_in, 16)
            for i, (grp, side, j, _, _) in enumerate(tiles):
                if side == "a":
                    pe.wait_ge(wa_in, 48)
                elif j == 0:
                    pe.wait_ge(w_in_sem[grp % WBUFS], 16 * (grp // WBUFS + 1))
                if i >= PROJ_BANKS:
                    pe.wait_ge((ev_act, ev_dve)[i % 2], (i - PROJ_BANKS) // 2 + 1)
                w = w_buf[grp % WBUFS]
                for k in range(KC):
                    if side == "w":
                        mm = t.matmul(bank[i % PROJ_BANKS][:], w[:, k, j * P:(j + 1) * P], xT_sb[:, k, :], start=k == 0, stop=k == KC - 1)
                    elif side == "x":
                        mm = t.matmul(bank[i % PROJ_BANKS][:], xT_sb[:, k, j * P:(j + 1) * P], w[:, k, :], start=k == 0, stop=k == KC - 1)
                    else:
                        mm = t.matmul(bank[i % PROJ_BANKS][0:RANK, :], wa_sb[:, k, :], xT_sb[:, k, :], start=k == 0, stop=k == KC - 1)
                mm.then_inc(proj_tile, 1)
                if i == U_AT:
                    pe.wait_ge(ev_act, 3)
                    for hp in range(2):
                        t.matmul(bank[6 + hp][:], wg_sb[:, hp * P:(hp + 1) * P], aT, start=True, stop=True).then_inc(u_ready, 1)
                if i == KST_AT:
                    pe.wait_ge(qk_ready, 1)
                    pe.wait_ge(made, 1)
                    for b in range(NB):
                        for hp in range(2):
                            n = 2 * b + hp
                            mm = t.transpose(bank[6 + n // 4][:, (n % 4) * P:(n % 4 + 1) * P], kgT[:, hp, b * P:(b + 1) * P], ident[:])
                            if n % 4 == 3:
                                mm.then_inc(kst_T, 1)
                c = i - SU_AT
                if 0 <= c < 7:
                    pe.wait_ge(kst_copied, 2)
                    if c >= 2:
                        pe.wait_ge(st_ready, c - 1)
                    b, r = c // 2, (c % 2) * GC
                    for h in range(GH):
                        hp, q = h // 2, (h % 2) * GDK
                        mm = t.matmul(bank[6 + c % 2][q:q + GDK, hp * GDV:(hp + 1) * GDV], kstT[r:r + GC, b, hp, q:q + GDK],
                                      vg[r:r + GC, b, h * GDV:(h + 1) * GDV], start=True, stop=True)
                    mm.then_inc(su_ready, 1)

            pe.wait_ge(ev_act, (NT + 1) // 2)
            pe.wait_ge(ev_dve, NT // 2)
            pe.wait_ge(st_ready, 7)

            def z(n):
                b, par, c = sb_tiles[n]
                r = par * SD
                if n >= ZB:
                    pe.wait_ge(w_exp, n - ZB + 1)
                for j in range(4):
                    mm = t.matmul(bank[n % ZB][:, j * P:(j + 1) * P], ksT[r:r + SD, j, c * P:(c + 1) * P],
                                  qsT[r:r + SD, j, b * P:(b + 1) * P], start=j == 0, stop=False, skip_group_check=True)
                mm.then_inc(z_ready, 1)

            def tail_sums(n):
                b, par, c = sb_tiles[n]
                pe.wait_ge(sp_ready, n + 1)
                for m in range(first[b, par], n):
                    t.matmul(bank[n % ZB][:], neg_one[:], sp[:, m % SP_BUFS, :], start=False, stop=False, skip_group_check=True)
                t.matmul(bank[n % ZB][:], neg_tri[:], sp[:, n % SP_BUFS, :], start=False, stop=True,
                         skip_group_check=True).then_inc(zc_ready, 1)

            def att(b):
                if b:
                    pe.wait_ge(go_ready, b)
                    pe.wait_ge(o_copied, 3 * b)
                for h in range(GH):
                    hp, par = h // 2, h % 2
                    q = par * GDK
                    mm = t.matmul(bank[4 + par][:, hp * P:(hp + 1) * P], kin[q:q + GDK, hp, b * P:(b + 1) * P],
                                  qgT[q:q + GDK, hp, b * P:(b + 1) * P], start=True, stop=True)
                mm.then_inc(att_ready, 1)

            def values_out(b, par):
                pe.wait_ge(w_exp, last[b, par] + 1)
                pe.wait_ge(w_masked, 2 * b + par + 1)
                for j in range(4):
                    h = 2 * j + par
                    for c in range(b + 1):
                        n = first[b, par] + b - c
                        mm = t.matmul(bank[3][:, h * SD:(h + 1) * SD], wT[:, n % W_BUFS, j * P:(j + 1) * P],
                                      vs[:, c, h * SD:(h + 1) * SD], start=c == 0, stop=c == b)
                mm.then_inc(av_ready, 1)

            def heads_out(b):
                values_out(b, 1)
                pe.wait_ge(attm_ready, b + 1)
                for h in range(GH):
                    hp, par = h // 2, h % 2
                    q, ob = par * GDK, bank[4 + par]
                    mm = t.matmul(ob[:, hp * GDV:(hp + 1) * GDV], attm[:, par, hp, :], vg[:, b, h * GDV:(h + 1) * GDV],
                                  start=True, stop=False, skip_group_check=True)
                    for r in range(2):
                        c = 2 * b + r
                        if c:
                            mm = t.matmul(ob[r * GC:(r + 1) * GC, hp * GDV:(hp + 1) * GDV],
                                          qgT[q:q + GDK, hp, c * GC:(c + 1) * GC], state[q:q + GDK, c, hp, :],
                                          start=False, stop=True, skip_group_check=True)
                mm.then_inc(go_ready, 1)

            def turn(b, i):
                if i:
                    pe.wait_ge(oT_copied, 2 * b + 1)
                else:
                    pe.wait_ge(on_ready, b + 1)
                    if b:
                        pe.wait_ge(mix_used, 2 * b)
                for k in range(4):
                    mm = t.transpose(bank[6][:, k * P:(k + 1) * P], o_n[:, (4 * i + k) * P:(4 * i + k + 1) * P], ident[:])
                mm.then_inc(oT_ready, 1)

            def mix(b, n):
                if n:
                    pe.wait_ge(mix_used, 2 * b + 1)
                else:
                    pe.wait_ge(oT_copied, 2 * (b + 1))
                    pe.wait_ge(wo_in, 16)
                for k in range(KC):
                    mm = t.matmul(bank[6][:], oT[:, k, :], wo_sb[:, k, n * 512:(n + 1) * 512], start=k == 0, stop=k == KC - 1)
                mm.then_inc(mix_part, 1)

            def transpose_x1(b, i, bk):
                pe.wait_ge(x1_ready, b + 1)
                if b == 0 and i:
                    pe.wait_ge(x1T_copied, 1)
                for k in range(4 * i, 4 * i + 4):
                    mm = t.transpose(bank[bk][:, (k % 4) * P:(k % 4 + 1) * P], x_sb[:, b, k * P:(k + 1) * P], ident[:])
                mm.then_inc(x1T_done, 1)

            def query(h, u0, w, lo):
                pe.wait_ge(sc_copied, h + (u0 + 1))
                for k in range(KC):
                    mm = t.matmul(bank[7][:, 0:QW], x1T[:, k, :], w[:, k, lo], start=k == 0, stop=k == KC - 1)
                mm.then_inc(q_done, 1)

            def query_T(h, u0):
                pe.wait_ge(q_copied, h + (u0 + 1))
                for s in range(2):
                    mm = t.transpose(bank[7][:, s * P:(s + 1) * P], q_sb[:, s * P:(s + 1) * P], ident[:])
                mm.then_inc(qT_done, 1)

            def scores(h, u0):
                pe.wait_ge(qT_copied, h + (u0 + 1))
                for s in range(2):
                    mm = t.matmul(bank[7][:, s * P:(s + 1) * P], qT_sb[:, s, :],
                                  keys[:, (bass.ds(h * QW + s * P, P) if not isinstance(h, int) else slice(h * QW + s * P, h * QW + s * P + P))],
                                  start=True, stop=True)
                mm.then_inc(sc_done, 1)

            for step, arg in plan:
                if step == "z":
                    z(arg)
                elif step == "tail_sums":
                    tail_sums(arg)
                elif step == "values_out":
                    if arg:
                        pe.wait_ge(o_copied, 3 * arg)
                    values_out(arg, 0)
                elif step == "att":
                    att(arg)
                elif step == "heads_out":
                    heads_out(arg)
                elif step == "turn":
                    turn(*arg)
                elif step == "mix":
                    mix(*arg)
                elif step == "turn_x1":
                    transpose_x1(0, arg, 7)
                elif step == "query":
                    if arg == 0:
                        pe.wait_ge(keys_in, 16)
                        pe.wait_ge(x1T_copied, 2)
                    pe.wait_ge(wq_head_in[arg % 2], 16 * (arg // 2 + 1))
                    query(arg, 0, wq_buf[arg % 2], slice(0, QW))
                elif step == "query_T":
                    query_T(arg, 0)
                elif step == "scores":
                    scores(arg, 0)

            def values(h, b, grp):
                half = grp % 2
                for k in range(GROUP):
                    s = half * GROUP + k
                    pe.wait_ge(diag_done, h * TOPK + (b * SLOTS + grp * GROUP + k + 1))
                    for n in range(2):
                        mm = t.matmul(bank[2 * (b % 2) + n][:], diag[:, s, :], rows[s][:, D + n * 512:D + (n + 1) * 512],
                                      start=False, stop=False, skip_group_check=True)
                    mm.then_inc(v_done, 1)

            pe.wait_ge(filled, 1)
            pe.wait_ge(o_copied, 3 * NB)
            for b in range(2):
                for n in range(2):
                    t.matmul(bank[2 * b + n][:], zeros[:, 0:P], zeros, start=True, stop=False, skip_group_check=True).then_inc(v_done, RING // 4)
            pe.wait_ge(wq_in, 16)
            for b in range(NB):
                if b >= 2:
                    pe.wait_ge(ffn_done, b - 1)
                    for n in range(2):
                        t.matmul(bank[2 * (b % 2) + n][:], zeros[:, 0:P], zeros, start=True, stop=False, skip_group_check=True)
                if b < NB - 1:
                    for i in range(2):
                        transpose_x1(b + 1, i, 5 + i)
                    pe.wait_ge(x1T_copied, 2 * (b + 2))
                with pe.Fori(0, PH) as h:
                    u0 = (b + 1) * PH
                    route = b < NB - 1
                    if route:
                        query(h, u0, wq_sb, bass.ds(h * QW, QW))
                    values(h, b, 0)
                    if route:
                        query_T(h, u0)
                    values(h, b, 1)
                    if route:
                        scores(h, u0)
                    values(h, b, 2)
                    values(h, b, 3)

        @block.scalar
        def _(act):
            a = nc.scalar
            st = Steps(act, act_steps)
            act.preload_act_table_set("natural_log_exp_and_others")
            for i, (_, side, _, dst, scale) in enumerate(tiles):
                if i % 2 == 0:
                    act.wait_ge(proj_tile, i + 1)
                    src = bank[i % PROJ_BANKS][0:RANK, :] if side == "a" else bank[i % PROJ_BANKS][:]
                    a.activation(dst, src, ACT.Copy, scale=scale).then_inc(ev_act, 1)
                j = (i - SILU_AT) // 2
                if i % 2 == 0 and 0 <= j < NB:
                    tile = 4 * W_GROUPS.index(C_GG) + 1 + j
                    act.wait_ge((ev_act, ev_dve)[tile % 2], tile // 2 + 1)
                    if j >= 2:
                        act.wait_ge(silu_done, j - 1)
                    st(a.activation(sig[:, j % 2, :], gg[:, j, :], ACT.Abs))
                    st.wait()
                    st(a.activation(sig[:, j % 2, :], sig[:, j % 2, :], ACT.Exp, scale=-1.0))
                    st.wait()
                    a.activation(sig[:, j % 2, :], sig[:, j % 2, :], ACT.Ln, bias=1.0).then_inc(sig_log, 1)
                if i % 2 == 0 and 0 <= j - 1 < NB:
                    act.wait_ge(sig_sum, j)
                    a.activation(sig[:, (j - 1) % 2, :], sig[:, (j - 1) % 2, :], ACT.Exp).then_inc(sig_exp, 1)
                if i == U_AT:
                    for hp in range(2):
                        act.wait_ge(u_ready, hp + 1)
                        a.activation(t1[:, hp, :], bank[6 + hp][:], ACT.Abs, bias=bg_sb[:, hp:hp + 1]).then_inc(uabs, 1)
                    act.wait_ge(uabs, 2)
                    st(a.activation(t1, t1, ACT.Exp, scale=-1.0))
                    st.wait()
                    a.activation(t1, t1, ACT.Ln, bias=1.0).then_inc(uexp, 1)
                if i == U_AT + 2:
                    act.wait_ge(cumd, 2)
                    a.activation(ecum, cum, ACT.Exp, scale=1.0 / GATE_TEMP).then_inc(ecumd, 1)
                    a.activation(t1, cum, ACT.Exp, scale=-1.0 / GATE_TEMP).then_inc(ecumd, 1)
                    act.wait_ge(dlast, 1)
                    a.activation(t2, t2, ACT.Exp, scale=1.0 / GATE_TEMP).then_inc(kst_exp, 1)
                if i == KST_AT:
                    for n in range(2):
                        act.wait_ge(kst_T, n + 1)
                        a.activation(kstT[:, 2 * n:2 * n + 2], bank[6 + n][:].rearrange("p (b h n) -> p b h n", b=2, h=2),
                                     ACT.Copy).then_inc(kst_copied, 1)
            act.wait_ge(st_ready, 7)

            def softplus_log(n):
                act.wait_ge(z_ready, n + 1)
                if n >= SP_BUFS:
                    b, par, _ = sb_tiles[n - SP_BUFS]
                    act.wait_ge(zc_ready, last[b, par] + 1)
                buf = sp[:, n % SP_BUFS, :]
                st(a.activation(buf, bank[n % ZB][:], ACT.Abs))
                st.wait()
                st(a.activation(buf, buf, ACT.Exp, scale=-1.0))
                st.wait()
                a.activation(buf, buf, ACT.Ln, bias=1.0).then_inc(l_ready, 1)

            def weights(n):
                b, par, c = sb_tiles[n]
                if n >= W_BUFS:
                    b2, par2, _ = sb_tiles[n - W_BUFS]
                    act.wait_ge(av_ready, 2 * b2 + par2 + 1)
                if c == b:
                    act.wait_ge(zmin_ready, 2 * b + par + 1)
                    a.activation(wT[:, n % W_BUFS, :], zmin, ACT.Exp).then_inc(w_exp, 1)
                else:
                    act.wait_ge(zc_ready, n + 1)
                    a.activation(wT[:, n % W_BUFS, :], bank[n % ZB][:], ACT.Exp).then_inc(w_exp, 1)

            def copy_heads(b):
                act.wait_ge(av_ready, 2 * (b + 1))
                if b:
                    act.wait_ge(oT_ready, 2 * b)
                a.activation(o_n[:, 512:1024], bank[3][:], ACT.Copy).then_inc(o_copied, 1)
                act.wait_ge(go_ready, b + 1)
                o_v = o_n[:, 0:512].rearrange("p (h r n) -> p h r n", h=2, r=2)
                for par in range(2):
                    a.activation(o_v[:, :, par, :], bank[4 + par][:, 0:256].rearrange("p (h n) -> p h n", h=2),
                                 ACT.Copy).then_inc(o_copied, 1)

            def head_roots(b):
                act.wait_ge(ms_ready, b + 1)
                st(a.activation(ms[:], ms[:], ACT.Ln))
                st.wait()
                a.activation(ms[:], ms[:], ACT.Exp, scale=-0.5).then_inc(rs_ready, 1)

            def copy_oT(b, i):
                act.wait_ge(oT_ready, 2 * b + i + 1)
                if b:
                    act.wait_ge(mix_part, 2 * b)
                a.activation(oT[:, 4 * i:4 * i + 4, :], bank[6][:].rearrange("p (k n) -> p k n", k=4),
                             ACT.Copy).then_inc(oT_copied, 1)

            def root(b, var_sem, root_sem):
                act.wait_ge(var_sem, b + 1)
                st(a.activation(rstd[:], rstd[:], ACT.Ln))
                st.wait()
                a.activation(rstd[:], rstd[:], ACT.Exp, scale=-0.5).then_inc(root_sem, 1)

            def copy_x1T(b, i, bk):
                act.wait_ge(x1T_done, 2 * b + i + 1)
                if b:
                    act.wait_ge(q_done, b * PH)
                a.activation(x1T[:, 4 * i:4 * i + 4, :], bank[bk][:].rearrange("p (k n) -> p k n", k=4),
                             ACT.Copy).then_inc(x1T_copied, 1)

            def copy_q(h, u0):
                act.wait_ge(q_done, h + (u0 + 1))
                a.activation(q_sb, bank[7][:, 0:QW], ACT.Copy).then_inc(q_copied, 1)

            def copy_qT(h, u0):
                act.wait_ge(qT_done, h + (u0 + 1))
                a.activation(qT_sb, bank[7][:, 0:QW].rearrange("p (s n) -> p s n", s=2), ACT.Copy).then_inc(qT_copied, 1)

            def gate_exp(h, u0):
                act.wait_ge(best_ready, h + (u0 + 1))
                a.activation(eb, best, ACT.Exp, bias=nbest, accum_out=esum).then_inc(gexp, 1)

            for step, arg in plan:
                if step == "sp":
                    softplus_log(arg)
                elif step == "w":
                    weights(arg)
                elif step == "copy_heads":
                    copy_heads(arg)
                elif step == "head_roots":
                    head_roots(arg)
                elif step == "copy_oT":
                    copy_oT(*arg)
                elif step == "root":
                    root(arg, var1, rstd1)
                elif step == "copy_x1T":
                    copy_x1T(0, arg, 7)
                elif step == "copy_q":
                    copy_q(arg, 0)
                elif step == "copy_qT":
                    copy_qT(arg, 0)
                elif step == "gate_exp":
                    gate_exp(arg, 0)

            def gelu(h, b, grp):
                act.wait_ge(dot_done, h * GROUPS + (b * PH * GROUPS + grp + 1))
                a.activation(acts[:, grp % 2, :], dots[:, grp % 2, :], ACT.Gelu).then_inc(gelu_done, 1)

            def diagonals(h, b, grp):
                act.wait_ge(w_done, h * GROUPS + (b * PH * GROUPS + grp + 2))
                act.wait_ge(v_done, h * TOPK + (b * SLOTS + (grp + 1) * GROUP))
                for k in range(GROUP):
                    s = (grp % 2) * GROUP + k
                    a.activation(diag[:, s, :], ident[:], ACT.Copy, scale=wts[:, grp % 2, k:k + 1]).then_inc(diag_done, 1)

            for b in range(NB):
                route = b < NB - 1
                if route:
                    for i in range(2):
                        copy_x1T(b + 1, i, 5 + i)
                with act.Fori(0, PH) as h:
                    u0 = (b + 1) * PH
                    gelu(h, b, 0)
                    diagonals(h, b, 0)
                    if route:
                        copy_q(h, u0)
                    gelu(h, b, 1)
                    diagonals(h, b, 1)
                    if route:
                        copy_qT(h, u0)
                    gelu(h, b, 2)
                    diagonals(h, b, 2)
                    gelu(h, b, 3)
                    diagonals(h, b, 3)
                    if route:
                        gate_exp(h, u0)
                root(b, var2, rstd2)

        @block.vector
        def _(dve):
            v = nc.vector
            st = Steps(dve, dve_steps)
            dve.sem_inc(sc_copied, 1)

            def decay_sums():
                for hp in range(2):
                    dve.wait_ge(uabs, hp + 1)
                    st(v.tensor_scalar(t2[:, hp, :], bank[6 + hp][:], bg_sb[:, hp:hp + 1], 0.0, ALU.add, ALU.min))
                st.wait()
                dve.wait_ge(uexp, 1)
                st(v.tensor_tensor(t2, t2, t1, ALU.subtract))
                st.wait()
                dve.wait_ge(made, 1)
                for hp in range(2):
                    v.tensor_tensor_scan(cum[:, hp, :], carry, t2[:, hp, :], 0.0, ALU.mult, ALU.add).then_inc(cumd, 1)
                dve.wait_ge(cumd, 2)
                for hp in range(2):
                    c_v = cum[:, hp, :].rearrange("p (c t) -> p c t", t=GC)
                    ins = v.tensor_tensor(t2[:, hp, :].rearrange("p (c t) -> p c t", t=GC),
                                          c_v[:, :, GC - 1:GC].to_broadcast([P, SEQ // GC, GC]), c_v, ALU.subtract)
                ins.then_inc(dlast, 1)

            def decayed_keys():
                dve.wait_ge(ecumd, 2)
                dve.wait_ge(ev_act, 2)
                dve.wait_ge(ev_dve, 2)
                st(v.tensor_tensor(kin, kgT, t1, ALU.mult))
                st(v.scalar_tensor_tensor(out=qgT, in0=qgT, scalar=GDK ** -0.5, in1=ecum, op0=ALU.mult, op1=ALU.mult))
                dve.wait_ge(kst_exp, 1)
                st.wait()
                v.tensor_tensor(kgT, kgT, t2, ALU.mult).then_inc(qk_ready, 1)

            def next_state(c):
                dve.wait_ge(su_ready, c + 1)
                for hp in range(2):
                    su = bank[6 + c % 2][:, hp * GDV:(hp + 1) * GDV]
                    if c == 0:
                        ins = v.tensor_copy(state[:, 1, hp, :], su)
                    else:
                        if hp == 0:
                            dve.wait_ge(st_ready, c)
                        ins = v.scalar_tensor_tensor(out=state[:, c + 1, hp, :], in0=state[:, c, hp, :],
                                                     scalar=ecum[:, hp, (c + 1) * GC - 1:(c + 1) * GC], in1=su,
                                                     op0=ALU.mult, op1=ALU.add)
                ins.then_inc(st_ready, 1)

            for i, (_, side, _, dst, scale) in enumerate(tiles):
                if i % 2 == 1:
                    dve.wait_ge(proj_tile, i + 1)
                    src = bank[i % PROJ_BANKS][0:RANK, :] if side == "a" else bank[i % PROJ_BANKS][:]
                    v.tensor_scalar(dst, src, scale, None, ALU.mult).then_inc(ev_dve, 1)
                    j = (i - 1 - SILU_AT) // 2
                    if 0 <= j < NB:
                        dve.wait_ge(sig_log, j + 1)
                        tile = 4 * W_GROUPS.index(C_GG) + 1 + j
                        dve.wait_ge((ev_act, ev_dve)[tile % 2], tile // 2 + 1)
                        v.scalar_tensor_tensor(out=sig[:, j % 2, :], in0=gg[:, j, :], scalar=0.0, in1=sig[:, j % 2, :],
                                               op0=ALU.min, op1=ALU.subtract).then_inc(sig_sum, 1)
                    if 0 <= j - 1 < NB:
                        dve.wait_ge(sig_exp, j)
                        v.tensor_tensor(gg[:, j - 1, :], gg[:, j - 1, :], sig[:, (j - 1) % 2, :], ALU.mult).then_inc(silu_done, 1)
                    if i == U_AT + 1:
                        decay_sums()
                    if i == U_AT + 3:
                        decayed_keys()
                for c in range(7):
                    if i % 2 and SU_AT + c in (i - 1, i):
                        next_state(c)
            def variance(y, var_sem):
                for n in range(2):
                    st(v.bn_stats(stats[:, n, :], y[:, n * 512:(n + 1) * 512]))
                st.wait()
                st(v.bn_aggr(mv[:], stats[:]))
                st.wait()
                v.tensor_scalar(rstd[:], mv[:, 1:2], EPS, None, ALU.add).then_inc(var_sem, 1)

            def normalise(y, b, rstd_sem, done):
                dve.wait_ge(rstd_sem, b + 1)
                st(v.tensor_scalar(y, y, mv[:, 0:1], rstd[:], ALU.subtract, ALU.mult))
                st.wait()
                st(v.tensor_tensor(y, y, ln_sb[:, 0, :], ALU.mult))
                st.wait()
                v.tensor_tensor(y, y, ln_sb[:, 1, :], ALU.add).then_inc(done, 1)

            def softplus(n):
                b, par, c = sb_tiles[n]
                dve.wait_ge(l_ready, n + 1)
                buf = sp[:, n % SP_BUFS, :]
                ins = v.scalar_tensor_tensor(out=buf, in0=bank[n % ZB][:], scalar=0.0, in1=buf, op0=ALU.max, op1=ALU.add)
                if c == b:
                    st(ins)
                    st.wait()
                    s_v = buf.rearrange("p (j q) -> p j q", j=4)
                    ins = v.tensor_tensor(s_v, s_v, before[:, None, :].to_broadcast([P, 4, P]), ALU.mult)
                ins.then_inc(sp_ready, 1)

            def diagonal_weights(n):
                dve.wait_ge(zc_ready, n + 1)
                if n:
                    dve.wait_ge(w_exp, n)
                v.tensor_scalar(zmin, bank[n % ZB][:], 0.0, None, ALU.min).then_inc(zmin_ready, 1)

            def mask_att(b):
                dve.wait_ge(att_ready, b + 1)
                if b:
                    dve.wait_ge(go_ready, b)
                for par in range(2):
                    ins = v.tensor_tensor(attm[:, par], bank[4 + par][:, 0:256].rearrange("p (h t) -> p h t", h=2),
                                          chunk_mask[:, None, :].to_broadcast([P, 2, P]), ALU.mult)
                ins.then_inc(attm_ready, 1)

            def head_squares(b):
                dve.wait_ge(o_copied, 3 * (b + 1))
                st(v.tensor_tensor(sq, o_n, o_n, ALU.mult))
                st.wait()
                st(v.tensor_reduce(ms[:, 0:GH], sq[:, 0:512].rearrange("p (h n) -> p h n", h=GH), AX_X, ALU.add))
                st(v.tensor_reduce(ms[:, GH:], sq[:, 512:].rearrange("p (h n) -> p h n", h=SH), AX_X, ALU.add))
                st.wait()
                st(v.tensor_scalar(ms[:, 0:GH], ms[:, 0:GH], 1.0 / GDV, EPS, ALU.mult, ALU.add))
                st(v.tensor_scalar(ms[:, GH:], ms[:, GH:], 1.0 / SD, EPS, ALU.mult, ALU.add))
                st.wait()
                dve.sem_inc(ms_ready, 1)

            def gate_heads(b):
                dve.wait_ge(rs_ready, b + 1)
                og = o_n[:, 0:512].rearrange("p (h n) -> p h n", h=GH)
                os_ = o_n[:, 512:1024].rearrange("p (h n) -> p h n", h=SH)
                st(v.tensor_tensor(og, og, ms[:, 0:GH, None].to_broadcast([P, GH, GDV]), ALU.mult))
                st(v.tensor_tensor(os_, os_, ms[:, GH:, None].to_broadcast([P, SH, SD]), ALU.mult))
                st.wait()
                if b == 0:
                    dve.wait_ge(consts_in, 48)
                    dve.wait_ge(x_in, 16)
                st(v.tensor_tensor(o_n, o_n, gains_sb[:], ALU.mult))
                st.wait()
                dve.wait_ge(silu_done, NB)
                v.tensor_tensor(o_n[:, 0:512], o_n[:, 0:512], gg[:, b, :], ALU.mult).then_inc(on_ready, 1)

            def residual(b, n):
                dve.wait_ge(mix_part, 2 * b + n + 1)
                xs = x_sb[:, b, n * 512:(n + 1) * 512]
                v.scalar_tensor_tensor(out=xs, in0=xs, scalar=ALPHA, in1=bank[6][:], op0=ALU.mult, op1=ALU.add).then_inc(mix_used, 1)

            def copy_scores(h, u0):
                dve.wait_ge(sc_done, h + (u0 + 1))
                st(v.tensor_copy(sc, bank[7][:, 0:QW].rearrange("p (s n) -> p s n", s=2)))
                st.wait()
                dve.sem_inc(sc_copied, 1)

            def top16(src, src2, vals, where):
                st.wait()
                st(v.max(vals[:, 0:8], src))
                st.wait()
                st(v.max_index(where[:, 0:8], vals[:, 0:8], src))
                st(v.match_replace(src2, vals[:, 0:8], src, LOWEST))
                st.wait()
                st(v.max(vals[:, 8:16], src2))
                st.wait()
                st(v.max_index(where[:, 8:16], vals[:, 8:16], src2))

            def candidates(h, u0):
                st.wait()
                st(v.tensor_tensor(cand.rearrange("p (i j) -> p i j", i=TOPK),
                                   top[:, 0, :, None].to_broadcast([P, TOPK, TOPK]),
                                   top[:, 1, None, :].to_broadcast([P, TOPK, TOPK]), ALU.add))
                top16(cand, cand2, best, pos[:, 0, :])
                st.wait()
                v.tensor_scalar(nbest, best[:, 0:1], -1.0, None, ALU.mult).then_inc(best_ready, 1)

            def finish_route(h, b, u0):
                par = (b % 2) * SLOTS

                def head_cols(h, par):
                    return slice(h * TOPK + par, (h + 1) * TOPK + par) if isinstance(h, int) else bass.ds(h * TOPK + par, TOPK)

                st(v.tensor_scalar(pos[:, 1, :], pos[:, 0, :], TOPK - 1, None, ALU.bitwise_and))
                st(v.tensor_copy(topf, topi[:]))
                st.wait()
                st(v.tensor_scalar(pos[:, 0, :], pos[:, 0, :], 4, None, ALU.logical_shift_right))
                st.wait()
                st(v.tensor_copy(posf, pos[:]))
                st.wait()
                for s in range(2):
                    st(v.tensor_tensor(onehot[:, s], posf[:, s, :, None].to_broadcast([P, TOPK, TOPK]),
                                       iota16[:, None, :].to_broadcast([P, TOPK, TOPK]), ALU.is_equal))
                st.wait()
                for s in range(2):
                    st(v.tensor_tensor(onehot[:, s], onehot[:, s], topf[:, s, None, :].to_broadcast([P, TOPK, TOPK]), ALU.mult))
                st.wait()
                st(v.tensor_reduce(sel, onehot, AX_X, ALU.add))
                st.wait()
                st(v.scalar_tensor_tensor(out=idx[:, head_cols(h, par)], in0=sel[:, 0, :], scalar=float(NKEYS),
                                          in1=sel[:, 1, :], op0=ALU.mult, op1=ALU.add))
                dve.wait_ge(gexp, h + (u0 + 1))
                st(v.reciprocal(esum, esum))
                st.wait()
                st(v.tensor_scalar(gates[:, head_cols(h, par)], eb, esum, None, ALU.mult))
                st.wait()
                dve.sem_inc(routed, 1)

            for step, arg in plan:
                if step == "sp":
                    softplus(arg)
                elif step == "w":
                    if sb_tiles[arg][0] == sb_tiles[arg][2]:
                        diagonal_weights(arg)
                elif step == "mask_att":
                    mask_att(arg)
                elif step == "head_squares":
                    head_squares(arg)
                elif step == "gate_heads":
                    gate_heads(arg)
                elif step == "residual":
                    residual(*arg)
                elif step == "variance":
                    dve.wait_ge(mix_used, 2 * (arg + 1))
                    variance(x_sb[:, arg, :], var1)
                elif step == "normalise":
                    normalise(x_sb[:, arg, :], arg, rstd1, x1_ready)
                elif step == "copy_scores":
                    copy_scores(arg, 0)
                elif step == "top_a":
                    top16(sc[:, 0, :], sc2[:, 0, :], top[:, 0, :], topi[:, 0, :])
                elif step == "top_b":
                    top16(sc[:, 1, :], sc2[:, 1, :], top[:, 1, :], topi[:, 1, :])
                elif step == "best":
                    candidates(arg, 0)
                elif step == "routed":
                    finish_route(arg, 0, 0)

            v.memset(zeros, 0.0).then_inc(filled, 1)
            dve.sem_inc(w_done, 1)

            def dot(h, b, grp):
                half = grp % 2
                for k in range(GROUP):
                    s = half * GROUP + k
                    dve.wait_ge(landed[s], h * (16 * GROUPS // 2) + (16 * (b * PH * GROUPS // 2 + grp // 2 + 1)))
                    u = rows[s][:, 0:D]
                    ins = v.tensor_tensor_reduce(u, u, x_sb[:, b, :], 1.0, 0.0, ALU.mult, ALU.add, dots[:, half, k:k + 1])
                ins.then_inc(dot_done, 1)

            def weigh(h, b, grp):
                half = grp % 2
                dve.wait_ge(gelu_done, h * GROUPS + (b * PH * GROUPS + grp + 1))
                v.tensor_tensor(wts[:, half, :], acts[:, half, :], gate_now[:, grp * GROUP:(grp + 1) * GROUP],
                                ALU.mult).then_inc(w_done, 1)

            st.restart()
            for b in range(NB):
                route = b < NB - 1
                u0 = (b + 1) * PH
                with dve.Fori(0, PH) as h:
                    dot(h, b, 0)
                    dve.wait_ge(w_done, h * GROUPS + (b * PH * GROUPS + 1))
                    st(v.tensor_copy(gate_now, gates[:, bass.ds(h * TOPK + (b % 2) * SLOTS, TOPK)]))
                    st.wait()
                    weigh(h, b, 0)
                    dot(h, b, 1)
                    weigh(h, b, 1)
                    dot(h, b, 2)
                    if route:
                        copy_scores(h, u0)
                        top16(sc[:, 0, :], sc2[:, 0, :], top[:, 0, :], topi[:, 0, :])
                    weigh(h, b, 2)
                    dot(h, b, 3)
                    if route:
                        top16(sc[:, 1, :], sc2[:, 1, :], top[:, 1, :], topi[:, 1, :])
                    weigh(h, b, 3)
                    if route:
                        candidates(h, u0)
                        finish_route(h, b + 1, u0)
                    st.restart()
                dve.wait_ge(v_done, RING + (b + 1) * SLOTS)
                if b:
                    dve.wait_ge(stored, 16 * b)
                if b == 0:
                    dve.wait_ge(ln2_in, 32)
                for n in range(2):
                    st(v.scalar_tensor_tensor(out=y2[:, n * 512:(n + 1) * 512], in0=x_sb[:, b, n * 512:(n + 1) * 512],
                                              scalar=ALPHA, in1=bank[2 * (b % 2) + n][:], op0=ALU.mult, op1=ALU.add))
                st.wait()
                dve.sem_inc(ffn_done, 1)
                variance(y2, var2)
                normalise(y2, b, rstd2, y_ready)
                st.restart()


def kernel(**inputs):
    import numpy as _np
    import concourse.bacc as _bacc
    from concourse import mybir as _mybir
    from concourse.bass_utils import run_bass_kernel_spmd as _run

    i = {k: _np.asarray(v) for k, v in inputs.items()}
    x = i["x"].reshape(512, 1024)
    laid = {
        "x": x,
        "xT": x.T,
        "w_in": i["w_in"][0],
        "w_gate": i["w_gla_gate"][0],
        "b_gate": i["b_gla_gate"].reshape(2, 128).T,
        "gains": _np.concatenate([i["gla_norm_g"].reshape(512), i["sb_norm_g"].reshape(512)]),
        "w_out": i["w_out"][0],
        "ln": _np.stack([i[k].reshape(1024) for k in ("ln1_g", "ln1_b", "ln2_g", "ln2_b")]),
        "w_query": i["peer_w_query"][0],
        "keysT": i["peer_sub_keys"].reshape(16, 128, 128).transpose(2, 0, 1).reshape(128, 2048),
        "experts": _np.concatenate([i["peer_u"][0], i["peer_v"][0]], axis=1),
    }
    nc = _bacc.Bacc("TRN2", target_bir_lowering=False, num_devices=1)
    arrays, args = {}, []
    for name, a in laid.items():
        a = _np.ascontiguousarray(a)
        arrays[f"in_{name}_dram"] = a
        args.append(nc.dram_tensor(f"in_{name}_dram", a.shape, _mybir.dt.from_np(a.dtype), kind="ExternalInput").ap())
    args.append(nc.dram_tensor("out_0_dram", (512, 1024), _mybir.dt.float32, kind="ExternalOutput").ap())
    hybrid_layer(nc, *args)
    r = _run(nc, [arrays], core_ids=[0])
    return r.results[0]["out_0_dram"].reshape(1, 512, 1024)
```

```python
from contextlib import ExitStack

import concourse.bass as bass
from concourse import mybir

F32 = mybir.dt.float32
U32 = mybir.dt.uint32
ALU = mybir.AluOpType
ACT = mybir.ActivationFunctionType
AX_X = mybir.AxisListType.X

P = 128
D = 1024
SEQ = 512
NB = SEQ // P
KC = D // P
GH, GDK, GDV, GC = 4, 64, 128, 64
RANK = 16
GATE_TEMP = 16.0
SH, SD = 8, 64
PH, NKEYS, TOPK = 8, 128, 16
QW = 2 * P
SLOTS = PH * TOPK
ALPHA = 2.0 ** 0.25
EPS = 1e-5
LOWEST = -3.0e38

RING = 8
GROUP = 2
GROUPS = TOPK // GROUP
GBUFS = RING // GROUP
SP_BUFS, W_BUFS = 6, 8
ZB = 3
ROUTE_STEPS = [(0, 0, 0, 0), (0, 0, 0, 0), (2, 1, 1, 1), (1, 2, 1, 1)]
TAIL_STEPS = [(1, 1, 0, 1), (1, 1, 1, 1), (2, 2, 2, 2), (1, 1, 1, 1)]
LAST_STEPS = (3, 1)
SILU_AT = 14
PROJ_BANKS = 6
U_AT, KST_AT, SU_AT = 8, 12, 13

C_QK, C_VG, C_GG, C_A, C_QS, C_KS, C_VS = 0, 512, 1024, 1536, 1552, 2064, 2576
W_GROUPS = [C_QK, C_VG, C_GG, C_QS, C_KS, C_VS]
WBUFS = 3
PIECES = 4


class Steps:

    def __init__(self, eng, sem):
        self.eng, self.sem, self.n = eng, sem, 0

    def __call__(self, ins):
        self.n += 1
        ins.then_inc(self.sem, 1)

    def wait(self):
        self.eng.wait_ge(self.sem, self.n)

    def restart(self):
        if self.n:
            self.wait()
        self.eng.sem_clear(self.sem)
        self.n = 0


def hybrid_layer(nc, x, xT, w_in, w_gate, b_gate, gains, w_out, ln, w_query, keysT, experts, out):
    ctx = ExitStack()
    with ctx:
        def sb(name, shape, dt=F32):
            return ctx.enter_context(nc.sbuf_tensor(name, shape, dt))

        def sem(name):
            return ctx.enter_context(nc.semaphore(name))

        bank = [ctx.enter_context(nc.psum_tensor(f"bank{i}", [P, 512], F32)) for i in range(8)]

        x_sb = sb("x_sb", [P, NB, D])
        x1T = sb("x1T", [P, KC, P])
        ln_sb = sb("ln_sb", [P, 2, D])
        rt = sb("rt", [P, 2048])
        small = sb("small", [P, 480])
        gains_sb = sb("gains_sb", [P, D])
        ring = sb("ring", [P, RING * 2 * D])
        big = sb("big", [P, KC * PH * QW])
        keys = sb("keys", [P, 2 * PH * NKEYS])
        scr = sb("scr", [P, 6144])
        ident = sb("ident", [P, P])
        neg_tri = sb("neg_tri", [P, P])
        neg_one = sb("neg_one", [P, P])
        before = sb("before", [P, P])
        chunk_mask = sb("chunk_mask", [P, P])
        iota16 = sb("iota16", [P, TOPK])
        bg_sb = sb("bg_sb", [P, 2])
        stats = sb("stats", [P, 2, 6])
        mv = sb("mv", [P, 2])
        rstd = sb("rstd", [P, 1])
        ms = sb("ms", [P, GH + SH])

        xT_sb = ring[:, 0:KC * SEQ].rearrange("p (k t) -> p k t", k=KC)
        w_buf = [ring[:, (i + 1) * 4096:(i + 2) * 4096].rearrange("p (k n) -> p k n", k=KC)
                 for i in range(WBUFS)]
        wa_sb = scr[:, 4096:4096 + KC * RANK].rearrange("p (k n) -> p k n", k=KC)
        wg_sb = scr[0:RANK, 4096 + KC * RANK:4096 + KC * RANK + 256]
        qgT = big[:, 0:1024].rearrange("p (h t) -> p h t", h=2)
        kgT = big[:, 1024:2048].rearrange("p (h t) -> p h t", h=2)
        qsT = big[:, 2048:4096].rearrange("p (h t) -> p h t", h=4)
        ksT = big[:, 4096:6144].rearrange("p (h t) -> p h t", h=4)
        vg = big[:, 6144:8192].rearrange("p (b n) -> p b n", b=NB)
        gg = big[:, 8192:10240].rearrange("p (b n) -> p b n", b=NB)
        vs = big[:, 10240:12288].rearrange("p (b n) -> p b n", b=NB)
        aT = big[0:RANK, 12288:12800]
        kin = big[:, 12800:13824].rearrange("p (h t) -> p h t", h=2)
        oT = big[:, 13824:14848].rearrange("p (k t) -> p k t", k=KC)
        attm = big[:, 14848:15360].rearrange("p (r h t) -> p r h t", r=2, h=2)
        carry = big[:, 15360:15872]
        wo_sb = ring[:, 8192:16384].rearrange("p (k n) -> p k n", k=KC)
        wT = ring[:, 4096:8192].rearrange("p (c n) -> p c n", c=W_BUFS)
        wq_pair = ring[:, 0:4096].rearrange("p (k n) -> p k n", k=KC)
        q_pair = scr[:, 3584:4096]
        o_n = big[:, 1024:2048]
        sig = rt[:, 1024:2048].rearrange("p (j n) -> p j n", j=2)
        kstT = rt[:, 0:1024].rearrange("p (b h n) -> p b h n", b=NB, h=2)
        cum = scr[:, 0:1024].rearrange("p (h t) -> p h t", h=2)
        ecum = scr[:, 1024:2048].rearrange("p (h t) -> p h t", h=2)
        t1 = scr[:, 2048:3072].rearrange("p (h t) -> p h t", h=2)
        t2 = scr[:, 3072:4096].rearrange("p (h t) -> p h t", h=2)
        state = scr[:, 4096:6144].rearrange("p (c h n) -> p c h n", c=8, h=2)
        sp = scr[:, 0:3072].rearrange("p (c n) -> p c n", c=SP_BUFS)
        zmin = scr[:, 3072:3584]
        sq = big[:, 15360:16384]
        wq_sb = big[:, :].rearrange("p (k n) -> p k n", k=KC)
        rows = [ring[:, i * 2 * D:(i + 1) * 2 * D] for i in range(RING)]
        q_sb = rt[:, 0:256]
        qT_sb = rt[:, 256:512].rearrange("p (s t) -> p s t", s=2)
        sc = rt[:, 512:768].rearrange("p (s n) -> p s n", s=2)
        sc2 = rt[:, 768:1024].rearrange("p (s n) -> p s n", s=2)
        cand = rt[:, 1024:1280]
        cand2 = rt[:, 1280:1536]
        onehot = rt[:, 1536:2048].rearrange("p (s k a) -> p s k a", s=2, k=TOPK)
        gates = small[:, 0:256]
        top = small[:, 256:288].rearrange("p (s k) -> p s k", s=2)
        topf = small[:, 288:320].rearrange("p (s k) -> p s k", s=2)
        posf = small[:, 320:352].rearrange("p (s k) -> p s k", s=2)
        sel = small[:, 352:384].rearrange("p (s k) -> p s k", s=2)
        best = small[:, 384:400]
        eb = small[:, 400:416]
        nbest = small[:, 416:417]
        esum = small[:, 417:418]
        gate_now = small[:, 424:440]
        dots = small[:, 440:448]
        acts = small[:, 448:456]
        wts = small[:, 456:464]
        diag = scr[:, 0:1024].rearrange("p (s n) -> p s n", s=RING)
        y2 = [scr[:, i * D:(i + 1) * D] for i in (1, 2)]
        zeros = zmin
        topi = sb("topi", [P, 2, TOPK], U32)
        pos = sb("pos", [P, 2, TOPK], U32)
        idx = sb("idx", [P, 2 * SLOTS], U32)
        idx_now = sb("idx_now", [P, RING], U32)

        wa_in, x_in, consts_in, wo_in, wq_in, keys_in, ln2_in = (
            sem(n) for n in ("wa_in", "x_in", "consts_in", "wo_in", "wq_in", "keys_in", "ln2_in"))
        wq_pair_in = sem("wq_pair_in")
        piece_in = [sem(f"piece_in{i}") for i in range(PIECES)]
        sig_log, sig_sum, sig_exp, silu_done = (sem(n) for n in ("sig_log", "sig_sum", "sig_exp", "silu_done"))
        mix_part, mix_used, gla_mixed = sem("mix_part"), sem("mix_used"), sem("gla_mixed")
        w_in_sem = [sem(f"w_in{i}") for i in range(WBUFS)]
        made, filled = sem("made"), sem("filled")
        proj_tile, ev_act, ev_dve = (sem(n) for n in ("proj_tile", "ev_act", "ev_dve"))
        act_steps, dve_steps, pool_steps = (sem(n) for n in ("act_steps", "dve_steps", "pool_steps"))
        u_ready, uabs, uexp, cumd, ecumd, kst_exp, dlast, qk_ready, kst_T, kst_copied, su_ready, st_ready = (
            sem(n) for n in ("u_ready", "uabs", "uexp", "cumd", "ecumd", "kst_exp", "dlast", "qk_ready",
                             "kst_T", "kst_copied", "su_ready", "st_ready"))
        z_ready, l_ready, sp_ready, zc_ready, zmin_ready, w_exp, w_masked, att_ready, attm_ready, av_ready, go_ready = (
            sem(n) for n in ("z_ready", "l_ready", "sp_ready", "zc_ready", "zmin_ready", "w_exp", "w_masked",
                             "att_ready", "attm_ready", "av_ready", "go_ready"))
        gla_copied, sb_copied, ms_ready, rs_ready, gated, oT_ready, oT_copied, var1, rstd1, x1_ready = (
            sem(n) for n in ("gla_copied", "sb_copied", "ms_ready", "rs_ready", "gated", "oT_ready", "oT_copied",
                             "var1", "rstd1", "x1_ready"))
        x1T_done, x1T_copied, q_done, q_copied, qT_done, qT_copied, sc_done, sc_copied, best_ready, gexp, routed = (
            sem(n) for n in ("x1T_done", "x1T_copied", "q_done", "q_copied", "qT_done", "qT_copied", "sc_done",
                             "sc_copied", "best_ready", "gexp", "routed"))
        landed = [sem(f"landed{i}") for i in range(RING)]
        dot_done, gelu_done, w_done, diag_done, v_done, ffn_done, var2, rstd2, y_ready = (
            sem(n) for n in ("dot_done", "gelu_done", "w_done", "diag_done", "v_done", "ffn_done", "var2", "rstd2",
                             "y_ready"))
        stored = [sem(f"stored{i}") for i in range(2)]

        tiles = []
        for g, c in enumerate(W_GROUPS):
            for j in range(4):
                if c == C_QK:
                    tiles.append((g, "w", j, (qgT, kgT)[j // 2][:, j % 2, :], 1.0))
                elif c == C_QS:
                    tiles.append((g, "w", j, qsT[:, j, :], SD ** -0.5))
                elif c == C_KS:
                    tiles.append((g, "w", j, ksT[:, j, :], 1.0))
                else:
                    tiles.append((g, "x", j, {C_VG: vg, C_GG: gg, C_VS: vs}[c][:, j, :], 1.0))
            if g == 0:
                tiles.append((0, "a", 0, aT, 1.0))
        NT = len(tiles)
        group_end = [max(i for i, tile in enumerate(tiles) if tile[0] == g) + 1 for g in range(len(W_GROUPS))]

        block = ctx.enter_context(nc.Block())

        sb_tiles = [(b, par, c) for b in range(NB) for par in range(2) for c in range(b, -1, -1)]
        NZ = len(sb_tiles)
        first = {}
        for n, (b, par, c) in enumerate(sb_tiles):
            first.setdefault((b, par), n)
        last = {(b, par): first[b, par] + b for b, par in first}

        def gla(b):
            last_mix = [("mix_gla", b)] * (b == NB - 1)
            return ([("gla_out", b), ("copy_gla", b), ("att", b + 1), ("squares", (b, 0)), ("mask_att", b + 1),
                     ("roots", (b, 0)), ("gate", (b, 0)), ("turn", (b, 0)), ("copy_oT", (b, 0))] + last_mix)

        def tail(b):
            clear = [("clear", 0)] * (b == NB - 1)
            return ([("copy_sb", b), ("squares", (b, 1))] + clear + [("roots", (b, 1)), ("gate", (b, 1)),
                     ("turn", (b, 1)), ("copy_oT", (b, 1)),
                     ("mix", (b, 0)), ("residual", (b, 0)), ("mix", (b, 1)), ("residual", (b, 1)),
                     ("variance", b), ("root", b), ("normalise", b)])

        def routing(h):
            make = [("query", h), ("copy_q", h)] * (h % 2 == 0) + [("query_T", h), ("copy_qT", h), ("scores", h), ("copy_scores", h)]
            choose = [("top", h - 1), ("best", h - 1), ("gate_exp", h - 1), ("routed", h - 1)]
            make, choose = make * (h < PH), choose * (h > 0)
            order = []
            for i in range(6):
                order += make[i:i + 1] + choose[i:i + 1]
            return order

        plan = [("z", 0), ("att", 0), ("mask_att", 0), ("z", 1), ("sp", 0)]
        tails, routes = gla(0), []

        def deal(n_tail, n_route):
            for _ in range(max(n_tail, n_route)):
                if n_tail > 0 and tails:
                    plan.append(tails.pop(0))
                    n_tail -= 1
                    if plan[-1] == ("normalise", 0):
                        routes.extend([("turn_x1", 0), ("copy_x1T", 0), ("turn_x1", 1), ("copy_x1T", 1)])
                        for h in range(PH + 1):
                            routes.extend(routing(h))
                if n_route > 0 and routes:
                    plan.append(routes.pop(0))
                    n_route -= 1

        for n, (b, par, c) in enumerate(sb_tiles):
            if n + 2 < NZ:
                plan.append(("z", n + 2))
            deal(TAIL_STEPS[b][0], ROUTE_STEPS[b][0])
            if n + 1 < NZ:
                plan.append(("sp", n + 1))
            deal(TAIL_STEPS[b][1], ROUTE_STEPS[b][1])
            plan.append(("tail_sums", n))
            if n == first[b, par] and (b or par):
                if par:
                    plan.append(("values_out", (b, 0)))
                else:
                    plan.append(("values_out", (b - 1, 1)))
                    tails.extend(tail(b - 1) + gla(b))
            deal(TAIL_STEPS[b][2], ROUTE_STEPS[b][2])
            plan.append(("w", n))
            deal(TAIL_STEPS[b][3], ROUTE_STEPS[b][3])
        plan.append(("values_out", (NB - 1, 1)))
        tails.extend(tail(NB - 1))
        while tails or routes:
            deal(*LAST_STEPS)
        plan = [step for step in plan if step not in (("att", NB), ("mask_att", NB))]

        def group_cols(grp):
            return slice(grp % GBUFS * GROUP, (grp % GBUFS + 1) * GROUP)

        @block.sync
        def _(sp_eng):
            xT_v = xT.rearrange("(k p) t -> p k t", p=P)
            w_v = w_in.rearrange("(k p) n -> p k n", p=P)
            for i in range(PIECES):
                ks = slice(i * KC // PIECES, (i + 1) * KC // PIECES)
                sp_eng.dma_start(xT_sb[:, ks, :], xT_v[:, ks, :]).then_inc(piece_in[i], 16)
                sp_eng.dma_start(w_buf[0][:, ks, :], w_v[:, ks, C_QK:C_QK + 512]).then_inc(piece_in[i], 16)
            for g, c in enumerate(W_GROUPS):
                if g >= WBUFS:
                    sp_eng.wait_ge(proj_tile, group_end[g - WBUFS])
                if g:
                    sp_eng.dma_start(w_buf[g % WBUFS], w_v[:, :, c:c + 512]).then_inc(w_in_sem[g % WBUFS], 16)
                if g == 0:
                    with nc.allow_non_contiguous_dma(reason="16 columns"):
                        sp_eng.dma_start(wa_sb, w_v[:, :, C_A:C_A + RANK]).then_inc(wa_in, 16)
                    sp_eng.dma_start(wg_sb, w_gate).then_inc(wa_in, 16)
                    sp_eng.dma_start(bg_sb[:], b_gate).then_inc(wa_in, 16)
            sp_eng.dma_start(x_sb[:], x.rearrange("(b p) d -> p b d", p=P)).then_inc(x_in, 16)
            sp_eng.dma_start(gains_sb[:], gains.partition_broadcast(P)).then_inc(consts_in, 16)
            for i in range(2):
                sp_eng.dma_start(ln_sb[:, i, :], ln[i:i + 1, :].rearrange("a d -> (a d)").partition_broadcast(P)).then_inc(consts_in, 16)
            sp_eng.wait_ge(proj_tile, NT)
            sp_eng.dma_start(wo_sb, w_out.rearrange("(k p) n -> p k n", p=P)).then_inc(wo_in, 16)
            wq_v = w_query.rearrange("(k p) n -> p k n", p=P)
            sp_eng.dma_start(keys[:], keysT).then_inc(keys_in, 16)
            for h in range(0, PH, 2):
                if h:
                    sp_eng.wait_ge(q_done, h)
                sp_eng.dma_start(wq_pair, wq_v[:, :, h * QW:(h + 2) * QW]).then_inc(wq_pair_in, 16)
            def wq_load(k, n=1):
                sp_eng.dma_start(wq_sb[:, k:k + n, :], wq_v[:, k:k + n, :]).then_inc(wq_in, 16)

            sp_eng.wait_ge(z_ready, NZ)
            wq_load(1, 2)
            sp_eng.wait_ge(go_ready, NB)
            wq_load(3)
            sp_eng.wait_ge(gated, 2 * NB - 1)
            wq_load(4)
            sp_eng.wait_ge(av_ready, 2 * NB)
            wq_load(5)
            sp_eng.wait_ge(oT_ready, 2 * NB)
            wq_load(0)
            sp_eng.wait_ge(mix_part, 2 * NB)
            wq_load(6, 2)
            sp_eng.wait_ge(x1_ready, NB)
            for i in range(2):
                sp_eng.dma_start(ln_sb[:, i, :], ln[2 + i:3 + i, :].rearrange("a d -> (a d)").partition_broadcast(P)).then_inc(ln2_in, 16)
            out_v = out.rearrange("(b p) d -> b p d", p=P)
            for b in range(NB):
                sp_eng.wait_ge(y_ready, b + 1)
                sp_eng.dma_start(out_v[b], y2[b % 2]).then_inc(stored[b % 2], 16)
            for i in range(2):
                sp_eng.wait_ge(stored[i], 16 * NB // 2)

        @block.gpsimd
        def _(pool):
            g = nc.gpsimd
            st = Steps(pool, pool_steps)
            g.memset(ident[:], 0.0)
            g.memset(neg_one[:], -1.0)
            g.memset(neg_tri[:], -1.0)
            g.memset(before[:], 1.0)
            g.memset(chunk_mask[:], 1.0)
            g.memset(carry, 1.0)
            st(g.iota(iota16[:], [[1, TOPK]], base=0, channel_multiplier=0, allow_small_or_imprecise_dtypes=True))
            st.wait()
            g.affine_select(out=ident[:], in_=ident[:], compare_op=ALU.not_equal, fill=1.0, base=0,
                            pattern=[[-1, P]], channel_multiplier=1)
            g.affine_select(out=neg_tri[:], in_=neg_tri[:], compare_op=ALU.is_ge, fill=0.0, base=0,
                            pattern=[[-1, P]], channel_multiplier=1)
            g.affine_select(out=before[:], in_=before[:], compare_op=ALU.is_gt, fill=0.0, base=0,
                            pattern=[[1, P]], channel_multiplier=-1)
            g.memset(carry.rearrange("p (c t) -> p c t", t=GC)[:, :, 0:1], 0.0)
            st(g.affine_select(out=chunk_mask[:], in_=chunk_mask[:], compare_op=ALU.is_ge, fill=0.0, base=0,
                               pattern=[[1, P]], channel_multiplier=-1))
            st.wait()
            g.affine_select(out=chunk_mask[:, GC:P], in_=chunk_mask[:, GC:P], compare_op=ALU.is_ge, fill=0.0, base=-GC,
                            pattern=[[0, GC]], channel_multiplier=1).then_inc(made, 1)
            for n, (b, _, c) in enumerate(sb_tiles):
                if c == b:
                    pool.wait_ge(w_exp, n + 1)
                    w_v = wT[:, n % W_BUFS, :].rearrange("p (j q) -> p j q", j=4)
                    g.tensor_tensor(w_v, w_v, before[:, None, :].to_broadcast([P, 4, P]), ALU.mult).then_inc(w_masked, 1)
            pool.wait_ge(q_done, PH)
            for b in range(NB):
                st.restart()
                with pool.Fori(0, PH) as h:
                    pool.wait_ge(routed, h + (b * PH + 1))
                    for i in range(TOPK):
                        s = i % RING
                        if b == 0 and i == 2:
                            pool.wait_ge(av_ready, 2 * NB)
                        if b == 0 and i == 4:
                            pool.wait_ge(gla_mixed, 1)
                        if b == 0 and i == 6:
                            pool.wait_ge(mix_part, 2 * NB)
                        pool.wait_ge(v_done, h * TOPK + (b * SLOTS + i + 1))
                        st(g.tensor_copy(idx_now[:, s:s + 1], idx[:, bass.ds(h * TOPK + ((b % 2) * SLOTS + i), 1)]))
                        st.wait()
                        g.indirect_dma_start(rows[s], None, experts, bass.IndirectOffsetOnAxis(
                            ap=idx_now[:, s:s + 1], axis=0)).then_inc(landed[s], 16)
                    st.restart()

        @block.tensor
        def _(pe):
            t = nc.tensor
            for k in range(KC):
                if k % (KC // PIECES) == 0:
                    pe.wait_ge(piece_in[k * PIECES // KC], 32)
                for j in range(4):
                    mm = t.matmul(bank[j][:], w_buf[0][:, k, j * P:(j + 1) * P], xT_sb[:, k, :], start=k == 0, stop=k == KC - 1)
                    if k == KC - 1:
                        mm.then_inc(proj_tile, 1)
            for i, (grp, side, j, _, _) in list(enumerate(tiles))[4:]:
                if side == "a":
                    pe.wait_ge(wa_in, 48)
                elif j == 0:
                    pe.wait_ge(w_in_sem[grp % WBUFS], 16 * (grp // WBUFS + (grp % WBUFS > 0)))
                if i >= PROJ_BANKS:
                    pe.wait_ge((ev_act, ev_dve)[i % 2], (i - PROJ_BANKS) // 2 + 1)
                w = w_buf[grp % WBUFS]
                for k in range(KC):
                    if side == "w":
                        mm = t.matmul(bank[i % PROJ_BANKS][:], w[:, k, j * P:(j + 1) * P], xT_sb[:, k, :], start=k == 0, stop=k == KC - 1)
                    elif side == "x":
                        mm = t.matmul(bank[i % PROJ_BANKS][:], xT_sb[:, k, j * P:(j + 1) * P], w[:, k, :], start=k == 0, stop=k == KC - 1)
                    else:
                        mm = t.matmul(bank[i % PROJ_BANKS][0:RANK, :], wa_sb[:, k, :], xT_sb[:, k, :], start=k == 0, stop=k == KC - 1)
                mm.then_inc(proj_tile, 1)
                if i == U_AT:
                    pe.wait_ge(ev_act, 3)
                    for hp in range(2):
                        t.matmul(bank[6 + hp][:], wg_sb[:, hp * P:(hp + 1) * P], aT, start=True, stop=True).then_inc(u_ready, 1)
                if i == KST_AT:
                    pe.wait_ge(qk_ready, 1)
                    pe.wait_ge(made, 1)
                    for b in range(NB):
                        for hp in range(2):
                            n = 2 * b + hp
                            mm = t.transpose(bank[6 + n // 4][:, (n % 4) * P:(n % 4 + 1) * P], kgT[:, hp, b * P:(b + 1) * P], ident[:])
                            if n % 4 == 3:
                                mm.then_inc(kst_T, 1)
                c = i - SU_AT
                if 0 <= c < 7:
                    pe.wait_ge(kst_copied, 2)
                    if c >= 2:
                        pe.wait_ge(st_ready, c - 1)
                    b, r = c // 2, (c % 2) * GC
                    for h in range(GH):
                        hp, q = h // 2, (h % 2) * GDK
                        mm = t.matmul(bank[6 + c % 2][q:q + GDK, hp * GDV:(hp + 1) * GDV], kstT[r:r + GC, b, hp, q:q + GDK],
                                      vg[r:r + GC, b, h * GDV:(h + 1) * GDV], start=True, stop=True)
                    mm.then_inc(su_ready, 1)

            pe.wait_ge(ev_act, (NT + 1) // 2)
            pe.wait_ge(ev_dve, NT // 2)
            pe.wait_ge(st_ready, 7)

            def z(n):
                b, par, c = sb_tiles[n]
                r = par * SD
                if n >= ZB:
                    pe.wait_ge(w_exp, n - ZB + 1)
                for j in range(4):
                    mm = t.matmul(bank[n % ZB][:, j * P:(j + 1) * P], ksT[r:r + SD, j, c * P:(c + 1) * P],
                                  qsT[r:r + SD, j, b * P:(b + 1) * P], start=j == 0, stop=False, skip_group_check=True)
                mm.then_inc(z_ready, 1)

            def tail_sums(n):
                b, par, c = sb_tiles[n]
                pe.wait_ge(sp_ready, n + 1)
                for m in range(first[b, par], n):
                    t.matmul(bank[n % ZB][:], neg_one[:], sp[:, m % SP_BUFS, :], start=False, stop=False, skip_group_check=True)
                t.matmul(bank[n % ZB][:], neg_tri[:], sp[:, n % SP_BUFS, :], start=False, stop=True,
                         skip_group_check=True).then_inc(zc_ready, 1)

            def att(b):
                if b:
                    pe.wait_ge(gla_copied, 2 * b)
                for h in range(GH):
                    hp, par = h // 2, h % 2
                    q = par * GDK
                    mm = t.matmul(bank[4 + par][:, hp * P:(hp + 1) * P], kin[q:q + GDK, hp, b * P:(b + 1) * P],
                                  qgT[q:q + GDK, hp, b * P:(b + 1) * P], start=True, stop=True)
                mm.then_inc(att_ready, 1)

            def values_out(b, par):
                pe.wait_ge(w_exp, last[b, par] + 1)
                pe.wait_ge(w_masked, 2 * b + par + 1)
                for j in range(4):
                    h = 2 * j + par
                    for c in range(b + 1):
                        n = first[b, par] + b - c
                        mm = t.matmul(bank[3][:, h * SD:(h + 1) * SD], wT[:, n % W_BUFS, j * P:(j + 1) * P],
                                      vs[:, c, h * SD:(h + 1) * SD], start=c == 0, stop=c == b)
                mm.then_inc(av_ready, 1)

            def gla_out(b):
                pe.wait_ge(attm_ready, b + 1)
                for h in range(GH):
                    hp, par = h // 2, h % 2
                    q, ob = par * GDK, bank[4 + par]
                    mm = t.matmul(ob[:, hp * GDV:(hp + 1) * GDV], attm[:, par, hp, :], vg[:, b, h * GDV:(h + 1) * GDV],
                                  start=True, stop=False, skip_group_check=True)
                    for r in range(2):
                        c = 2 * b + r
                        if c:
                            mm = t.matmul(ob[r * GC:(r + 1) * GC, hp * GDV:(hp + 1) * GDV],
                                          qgT[q:q + GDK, hp, c * GC:(c + 1) * GC], state[q:q + GDK, c, hp, :],
                                          start=False, stop=True, skip_group_check=True)
                mm.then_inc(go_ready, 1)

            def turn(b, i):
                pe.wait_ge(gated, 2 * b + i + 1)
                if i:
                    pe.wait_ge(oT_copied, 2 * b + 1)
                elif b:
                    pe.wait_ge(mix_used, 2 * b)
                for k in range(4):
                    mm = t.transpose(bank[6][:, k * P:(k + 1) * P], o_n[:, (4 * i + k) * P:(4 * i + k + 1) * P], ident[:])
                mm.then_inc(oT_ready, 1)

            def mix_gla(b):
                pe.wait_ge(oT_copied, 2 * b + 1)
                pe.wait_ge(gla_copied, 2 * (b + 1))
                pe.wait_ge(wo_in, 16)
                for n in range(2):
                    for k in range(KC // 2):
                        mm = t.matmul(bank[4 + n][:], oT[:, k, :], wo_sb[:, k, n * 512:(n + 1) * 512], start=k == 0, stop=False, skip_group_check=True)
                mm.then_inc(gla_mixed, 1)

            def mix(b, n):
                if b == NB - 1:
                    pe.wait_ge(oT_copied, 2 * (b + 1))
                    for k in range(KC // 2, KC):
                        mm = t.matmul(bank[4 + n][:], oT[:, k, :], wo_sb[:, k, n * 512:(n + 1) * 512], start=False, stop=k == KC - 1, skip_group_check=True)
                    mm.then_inc(mix_part, 1)
                    return
                if n:
                    pe.wait_ge(mix_used, 2 * b + 1)
                else:
                    pe.wait_ge(oT_copied, 2 * (b + 1))
                    pe.wait_ge(wo_in, 16)
                for k in range(KC):
                    mm = t.matmul(bank[6][:], oT[:, k, :], wo_sb[:, k, n * 512:(n + 1) * 512], start=k == 0, stop=k == KC - 1)
                mm.then_inc(mix_part, 1)

            def transpose_x1(b, i, bk):
                pe.wait_ge(x1_ready, b + 1)
                if b == 0 and i:
                    pe.wait_ge(x1T_copied, 1)
                for k in range(4 * i, 4 * i + 4):
                    mm = t.transpose(bank[bk][:, (k % 4) * P:(k % 4 + 1) * P], x_sb[:, b, k * P:(k + 1) * P], ident[:])
                mm.then_inc(x1T_done, 1)

            def query(h, u0, w, lo):
                pe.wait_ge(sc_copied, h + (u0 + 1))
                for k in range(KC):
                    mm = t.matmul(bank[7][:, 0:QW], x1T[:, k, :], w[:, k, lo], start=k == 0, stop=k == KC - 1)
                mm.then_inc(q_done, 1)

            def query_T(h, u0, q):
                pe.wait_ge(q_copied, h + (u0 + 1))
                pe.wait_ge(sc_copied, h + (u0 + 1))
                for s in range(2):
                    mm = t.transpose(bank[7][:, s * P:(s + 1) * P], q[:, s * P:(s + 1) * P], ident[:])
                mm.then_inc(qT_done, 1)

            def scores(h, u0):
                pe.wait_ge(qT_copied, h + (u0 + 1))
                for s in range(2):
                    mm = t.matmul(bank[7][:, s * P:(s + 1) * P], qT_sb[:, s, :],
                                  keys[:, (bass.ds(h * QW + s * P, P) if not isinstance(h, int) else slice(h * QW + s * P, h * QW + s * P + P))],
                                  start=True, stop=True)
                mm.then_inc(sc_done, 1)

            for step, arg in plan:
                if step == "z":
                    z(arg)
                elif step == "tail_sums":
                    tail_sums(arg)
                elif step == "values_out":
                    if arg[0] and not arg[1]:
                        pe.wait_ge(sb_copied, arg[0])
                    values_out(*arg)
                elif step == "att":
                    att(arg)
                elif step == "gla_out":
                    gla_out(arg)
                elif step == "mix_gla":
                    mix_gla(arg)
                elif step == "clear":
                    pe.wait_ge(filled, 1)
                    pe.wait_ge(w_exp, NZ)
                    pe.wait_ge(sb_copied, NB)
                    for n in range(4):
                        t.matmul(bank[n][:], zeros[:, 0:P], zeros, start=True, stop=False, skip_group_check=True)
                elif step == "turn":
                    turn(*arg)
                elif step == "mix":
                    mix(*arg)
                elif step == "turn_x1":
                    transpose_x1(0, arg, 7)
                elif step == "query":
                    if arg == 0:
                        pe.wait_ge(keys_in, 16)
                        pe.wait_ge(x1T_copied, 2)
                    pe.wait_ge(wq_pair_in, 16 * (arg // 2 + 1))
                    pe.wait_ge(sc_copied, arg + 1)
                    for k in range(KC):
                        mm = t.matmul(bank[7][:], x1T[:, k, :], wq_pair[:, k, :], start=k == 0, stop=k == KC - 1)
                    mm.then_inc(q_done, 2)
                elif step == "query_T":
                    query_T(arg, 0, q_pair[:, (arg % 2) * QW:(arg % 2 + 1) * QW])
                elif step == "scores":
                    scores(arg, 0)

            def values(h, b, grp):
                for k in range(GROUP):
                    s = (grp * GROUP + k) % RING
                    pe.wait_ge(diag_done, h * TOPK + (b * SLOTS + grp * GROUP + k + 1))
                    for n in range(2):
                        mm = t.matmul(bank[2 * (b % 2) + n][:], diag[:, s, :], rows[s][:, D + n * 512:D + (n + 1) * 512],
                                      start=False, stop=False, skip_group_check=True)
                    mm.then_inc(v_done, 1)

            pe.wait_ge(wq_in, 16 * 6)
            for b in range(NB):
                if b >= 2:
                    pe.wait_ge(ffn_done, b - 1)
                    for n in range(2):
                        t.matmul(bank[2 * (b % 2) + n][:], zeros[:, 0:P], zeros, start=True, stop=False, skip_group_check=True)
                if b < NB - 1:
                    for i in range(2):
                        if b == 0 and i:
                            pe.wait_ge(mix_used, 2 * NB)
                        transpose_x1(b + 1, i, 6 - i)
                    pe.wait_ge(x1T_copied, 2 * (b + 2))
                with pe.Fori(0, PH) as h:
                    u0 = (b + 1) * PH
                    route = b < NB - 1
                    if route:
                        query(h, u0, wq_sb, bass.ds(h * QW, QW))
                    for grp in range(GROUPS):
                        values(h, b, grp)
                        if route and grp == 1:
                            query_T(h, u0, q_sb)
                        elif route and grp == 3:
                            scores(h, u0)

        @block.scalar
        def _(act):
            a = nc.scalar
            st = Steps(act, act_steps)
            act.preload_act_table_set("natural_log_exp_and_others")
            for i, (_, side, _, dst, scale) in enumerate(tiles):
                if i % 2 == 0:
                    act.wait_ge(proj_tile, i + 1)
                    src = bank[i % PROJ_BANKS][0:RANK, :] if side == "a" else bank[i % PROJ_BANKS][:]
                    a.activation(dst, src, ACT.Copy, scale=scale).then_inc(ev_act, 1)
                j = (i - SILU_AT) // 2
                if i % 2 == 0 and 0 <= j < NB:
                    tile = 4 * W_GROUPS.index(C_GG) + 1 + j
                    act.wait_ge((ev_act, ev_dve)[tile % 2], tile // 2 + 1)
                    if j >= 2:
                        act.wait_ge(silu_done, j - 1)
                    st(a.activation(sig[:, j % 2, :], gg[:, j, :], ACT.Abs))
                    st.wait()
                    st(a.activation(sig[:, j % 2, :], sig[:, j % 2, :], ACT.Exp, scale=-1.0))
                    st.wait()
                    a.activation(sig[:, j % 2, :], sig[:, j % 2, :], ACT.Ln, bias=1.0).then_inc(sig_log, 1)
                if i % 2 == 0 and 0 <= j - 1 < NB:
                    act.wait_ge(sig_sum, j)
                    a.activation(sig[:, (j - 1) % 2, :], sig[:, (j - 1) % 2, :], ACT.Exp).then_inc(sig_exp, 1)
                if i == U_AT:
                    for hp in range(2):
                        act.wait_ge(u_ready, hp + 1)
                        a.activation(t1[:, hp, :], bank[6 + hp][:], ACT.Abs, bias=bg_sb[:, hp:hp + 1]).then_inc(uabs, 1)
                    act.wait_ge(uabs, 2)
                    st(a.activation(t1, t1, ACT.Exp, scale=-1.0))
                    st.wait()
                    a.activation(t1, t1, ACT.Ln, bias=1.0).then_inc(uexp, 1)
                if i == U_AT + 2:
                    act.wait_ge(cumd, 2)
                    a.activation(ecum, cum, ACT.Exp, scale=1.0 / GATE_TEMP).then_inc(ecumd, 1)
                    a.activation(t1, cum, ACT.Exp, scale=-1.0 / GATE_TEMP).then_inc(ecumd, 1)
                    act.wait_ge(dlast, 1)
                    a.activation(t2, t2, ACT.Exp, scale=1.0 / GATE_TEMP).then_inc(kst_exp, 1)
                if i == KST_AT:
                    for n in range(2):
                        act.wait_ge(kst_T, n + 1)
                        a.activation(kstT[:, 2 * n:2 * n + 2], bank[6 + n][:].rearrange("p (b h n) -> p b h n", b=2, h=2),
                                     ACT.Copy).then_inc(kst_copied, 1)
            act.wait_ge(st_ready, 7)

            def softplus_log(n):
                act.wait_ge(z_ready, n + 1)
                if n >= SP_BUFS:
                    b, par, _ = sb_tiles[n - SP_BUFS]
                    act.wait_ge(zc_ready, last[b, par] + 1)
                buf = sp[:, n % SP_BUFS, :]
                st(a.activation(buf, bank[n % ZB][:], ACT.Abs))
                st.wait()
                st(a.activation(buf, buf, ACT.Exp, scale=-1.0))
                st.wait()
                a.activation(buf, buf, ACT.Ln, bias=1.0).then_inc(l_ready, 1)

            def weights(n):
                b, par, c = sb_tiles[n]
                if n >= W_BUFS:
                    b2, par2, _ = sb_tiles[n - W_BUFS]
                    act.wait_ge(av_ready, 2 * b2 + par2 + 1)
                if c == b:
                    act.wait_ge(zmin_ready, 2 * b + par + 1)
                    a.activation(wT[:, n % W_BUFS, :], zmin, ACT.Exp).then_inc(w_exp, 1)
                else:
                    act.wait_ge(zc_ready, n + 1)
                    a.activation(wT[:, n % W_BUFS, :], bank[n % ZB][:], ACT.Exp).then_inc(w_exp, 1)

            def copy_gla(b):
                act.wait_ge(go_ready, b + 1)
                if b:
                    act.wait_ge(oT_ready, 2 * b - 1)
                o_v = o_n[:, 0:512].rearrange("p (h r n) -> p h r n", h=2, r=2)
                for par in range(2):
                    a.activation(o_v[:, :, par, :], bank[4 + par][:, 0:256].rearrange("p (h n) -> p h n", h=2),
                                 ACT.Copy).then_inc(gla_copied, 1)

            def copy_sb(b):
                act.wait_ge(av_ready, 2 * (b + 1))
                if b:
                    act.wait_ge(oT_ready, 2 * b)
                a.activation(o_n[:, 512:1024], bank[3][:], ACT.Copy).then_inc(sb_copied, 1)

            def roots(b, i):
                act.wait_ge(ms_ready, 2 * b + i + 1)
                m = ms[:, (slice(0, GH), slice(GH, GH + SH))[i]]
                st(a.activation(m, m, ACT.Ln))
                st.wait()
                a.activation(m, m, ACT.Exp, scale=-0.5).then_inc(rs_ready, 1)

            def copy_oT(b, i):
                act.wait_ge(oT_ready, 2 * b + i + 1)
                if b:
                    act.wait_ge(mix_part, 2 * b)
                a.activation(oT[:, 4 * i:4 * i + 4, :], bank[6][:].rearrange("p (k n) -> p k n", k=4),
                             ACT.Copy).then_inc(oT_copied, 1)

            def root(b, var_sem, root_sem):
                act.wait_ge(var_sem, b + 1)
                st(a.activation(rstd[:], rstd[:], ACT.Ln))
                st.wait()
                a.activation(rstd[:], rstd[:], ACT.Exp, scale=-0.5).then_inc(root_sem, 1)

            def copy_x1T(b, i, bk):
                act.wait_ge(x1T_done, 2 * b + i + 1)
                if b:
                    act.wait_ge(q_done, b * PH)
                a.activation(x1T[:, 4 * i:4 * i + 4, :], bank[bk][:].rearrange("p (k n) -> p k n", k=4),
                             ACT.Copy).then_inc(x1T_copied, 1)

            def copy_q(h, u0):
                act.wait_ge(q_done, h + (u0 + 1))
                a.activation(q_sb, bank[7][:, 0:QW], ACT.Copy).then_inc(q_copied, 1)

            def copy_qT(h, u0):
                act.wait_ge(qT_done, h + (u0 + 1))
                a.activation(qT_sb, bank[7][:, 0:QW].rearrange("p (s n) -> p s n", s=2), ACT.Copy).then_inc(qT_copied, 1)

            def gate_exp(h, u0):
                act.wait_ge(best_ready, h + (u0 + 1))
                a.activation(eb, best, ACT.Exp, bias=nbest, accum_out=esum).then_inc(gexp, 1)

            for step, arg in plan:
                if step == "sp":
                    softplus_log(arg)
                elif step == "w":
                    weights(arg)
                elif step == "copy_gla":
                    copy_gla(arg)
                elif step == "copy_sb":
                    copy_sb(arg)
                elif step == "roots":
                    roots(*arg)
                elif step == "copy_oT":
                    copy_oT(*arg)
                elif step == "root":
                    root(arg, var1, rstd1)
                elif step == "copy_x1T":
                    copy_x1T(0, arg, 7)
                elif step == "copy_q":
                    act.wait_ge(q_done, arg + 2)
                    if arg:
                        act.wait_ge(qT_done, arg)
                    a.activation(q_pair, bank[7][:], ACT.Copy).then_inc(q_copied, 2)
                elif step == "copy_qT":
                    copy_qT(arg, 0)
                elif step == "gate_exp":
                    gate_exp(arg, 0)

            def gelu(h, b, grp):
                act.wait_ge(dot_done, h * GROUPS + (b * PH * GROUPS + grp + 1))
                cols = group_cols(grp)
                a.activation(acts[:, cols], dots[:, cols], ACT.Gelu).then_inc(gelu_done, 1)

            def diagonals(h, b, grp):
                act.wait_ge(w_done, h * GROUPS + (b * PH * GROUPS + grp + 2))
                act.wait_ge(v_done, h * TOPK + (b * SLOTS + (grp + 1) * GROUP))
                for k in range(GROUP):
                    s = (grp * GROUP + k) % RING
                    a.activation(diag[:, s, :], ident[:], ACT.Copy, scale=wts[:, s:s + 1]).then_inc(diag_done, 1)

            for b in range(NB):
                route = b < NB - 1
                if route:
                    for i in range(2):
                        copy_x1T(b + 1, i, 6 - i)
                with act.Fori(0, PH) as h:
                    u0 = (b + 1) * PH
                    for grp in range(GROUPS):
                        gelu(h, b, grp)
                        diagonals(h, b, grp)
                        if route and grp == 1:
                            copy_q(h, u0)
                        elif route and grp == 3:
                            copy_qT(h, u0)
                    if route:
                        gate_exp(h, u0)
                for done in range(b - 1, b + (b == NB - 1)):
                    if done >= 0:
                        act.preload_act_table_set("natural_log_exp_and_others")
                        root(done, var2, rstd2)

        @block.vector
        def _(dve):
            v = nc.vector
            st = Steps(dve, dve_steps)
            dve.sem_inc(sc_copied, 1)
            dve.sem_inc(v_done, RING)

            def decay_sums():
                for hp in range(2):
                    dve.wait_ge(uabs, hp + 1)
                    st(v.tensor_scalar(t2[:, hp, :], bank[6 + hp][:], bg_sb[:, hp:hp + 1], 0.0, ALU.add, ALU.min))
                st.wait()
                dve.wait_ge(uexp, 1)
                st(v.tensor_tensor(t2, t2, t1, ALU.subtract))
                st.wait()
                dve.wait_ge(made, 1)
                for hp in range(2):
                    v.tensor_tensor_scan(cum[:, hp, :], carry, t2[:, hp, :], 0.0, ALU.mult, ALU.add).then_inc(cumd, 1)
                dve.wait_ge(cumd, 2)
                for hp in range(2):
                    c_v = cum[:, hp, :].rearrange("p (c t) -> p c t", t=GC)
                    ins = v.tensor_tensor(t2[:, hp, :].rearrange("p (c t) -> p c t", t=GC),
                                          c_v[:, :, GC - 1:GC].to_broadcast([P, SEQ // GC, GC]), c_v, ALU.subtract)
                ins.then_inc(dlast, 1)

            def decayed_keys():
                dve.wait_ge(ecumd, 2)
                dve.wait_ge(ev_act, 2)
                dve.wait_ge(ev_dve, 2)
                st(v.tensor_tensor(kin, kgT, t1, ALU.mult))
                st(v.scalar_tensor_tensor(out=qgT, in0=qgT, scalar=GDK ** -0.5, in1=ecum, op0=ALU.mult, op1=ALU.mult))
                dve.wait_ge(kst_exp, 1)
                st.wait()
                v.tensor_tensor(kgT, kgT, t2, ALU.mult).then_inc(qk_ready, 1)

            def next_state(c):
                dve.wait_ge(su_ready, c + 1)
                for hp in range(2):
                    su = bank[6 + c % 2][:, hp * GDV:(hp + 1) * GDV]
                    if c == 0:
                        ins = v.tensor_copy(state[:, 1, hp, :], su)
                    else:
                        if hp == 0:
                            dve.wait_ge(st_ready, c)
                        ins = v.scalar_tensor_tensor(out=state[:, c + 1, hp, :], in0=state[:, c, hp, :],
                                                     scalar=ecum[:, hp, (c + 1) * GC - 1:(c + 1) * GC], in1=su,
                                                     op0=ALU.mult, op1=ALU.add)
                ins.then_inc(st_ready, 1)

            for i, (_, side, _, dst, scale) in enumerate(tiles):
                if i % 2 == 1:
                    dve.wait_ge(proj_tile, i + 1)
                    src = bank[i % PROJ_BANKS][0:RANK, :] if side == "a" else bank[i % PROJ_BANKS][:]
                    v.tensor_scalar(dst, src, scale, None, ALU.mult).then_inc(ev_dve, 1)
                    j = (i - 1 - SILU_AT) // 2
                    if 0 <= j < NB:
                        dve.wait_ge(sig_log, j + 1)
                        tile = 4 * W_GROUPS.index(C_GG) + 1 + j
                        dve.wait_ge((ev_act, ev_dve)[tile % 2], tile // 2 + 1)
                        v.scalar_tensor_tensor(out=sig[:, j % 2, :], in0=gg[:, j, :], scalar=0.0, in1=sig[:, j % 2, :],
                                               op0=ALU.min, op1=ALU.subtract).then_inc(sig_sum, 1)
                    if 0 <= j - 1 < NB:
                        dve.wait_ge(sig_exp, j)
                        v.tensor_tensor(gg[:, j - 1, :], gg[:, j - 1, :], sig[:, (j - 1) % 2, :], ALU.mult).then_inc(silu_done, 1)
                    if i == U_AT + 1:
                        decay_sums()
                    if i == U_AT + 3:
                        decayed_keys()
                for c in range(7):
                    if i % 2 and SU_AT + c in (i - 1, i):
                        next_state(c)
            def variance(var_sem):
                st.wait()
                st(v.bn_aggr(mv[:], stats[:]))
                st.wait()
                v.tensor_scalar(rstd[:], mv[:, 1:2], EPS, None, ALU.add).then_inc(var_sem, 1)

            def normalise(y, b, rstd_sem, done):
                dve.wait_ge(rstd_sem, b + 1)
                st(v.tensor_scalar(y, y, mv[:, 0:1], rstd[:], ALU.subtract, ALU.mult))
                st.wait()
                st(v.tensor_tensor(y, y, ln_sb[:, 0, :], ALU.mult))
                st.wait()
                v.tensor_tensor(y, y, ln_sb[:, 1, :], ALU.add).then_inc(done, 1)

            def softplus(n):
                b, par, c = sb_tiles[n]
                dve.wait_ge(l_ready, n + 1)
                buf = sp[:, n % SP_BUFS, :]
                ins = v.scalar_tensor_tensor(out=buf, in0=bank[n % ZB][:], scalar=0.0, in1=buf, op0=ALU.max, op1=ALU.add)
                if c == b:
                    st(ins)
                    st.wait()
                    s_v = buf.rearrange("p (j q) -> p j q", j=4)
                    ins = v.tensor_tensor(s_v, s_v, before[:, None, :].to_broadcast([P, 4, P]), ALU.mult)
                ins.then_inc(sp_ready, 1)

            def diagonal_weights(n):
                dve.wait_ge(zc_ready, n + 1)
                if n:
                    dve.wait_ge(w_exp, n)
                v.tensor_scalar(zmin, bank[n % ZB][:], 0.0, None, ALU.min).then_inc(zmin_ready, 1)

            def mask_att(b):
                dve.wait_ge(att_ready, b + 1)
                if b:
                    dve.wait_ge(go_ready, b)
                for par in range(2):
                    ins = v.tensor_tensor(attm[:, par], bank[4 + par][:, 0:256].rearrange("p (h t) -> p h t", h=2),
                                          chunk_mask[:, None, :].to_broadcast([P, 2, P]), ALU.mult)
                ins.then_inc(attm_ready, 1)

            def squares(b, i):
                if i:
                    dve.wait_ge(sb_copied, b + 1)
                else:
                    dve.wait_ge(gla_copied, 2 * (b + 1))
                heads, width = ((GH, GDV), (SH, SD))[i]
                m = ms[:, i * GH:i * GH + heads]
                o_i, sq_i = o_n[:, i * 512:(i + 1) * 512], sq[:, i * 512:(i + 1) * 512]
                st(v.tensor_tensor(sq_i, o_i, o_i, ALU.mult))
                st.wait()
                st(v.tensor_reduce(m, sq_i.rearrange("p (h n) -> p h n", h=heads), AX_X, ALU.add))
                st.wait()
                v.tensor_scalar(m, m, 1.0 / width, EPS, ALU.mult, ALU.add).then_inc(ms_ready, 1)

            def gate(b, i):
                dve.wait_ge(rs_ready, 2 * b + i + 1)
                heads, width = ((GH, GDV), (SH, SD))[i]
                o_i = o_n[:, i * 512:(i + 1) * 512]
                o_v = o_i.rearrange("p (h n) -> p h n", h=heads)
                st(v.tensor_tensor(o_v, o_v, ms[:, i * GH:i * GH + heads, None].to_broadcast([P, heads, width]), ALU.mult))
                st.wait()
                if b == 0:
                    dve.wait_ge(consts_in, 48)
                    dve.wait_ge(x_in, 16)
                ins = v.tensor_tensor(o_i, o_i, gains_sb[:, i * 512:(i + 1) * 512], ALU.mult)
                if i == 0:
                    st(ins)
                    st.wait()
                    dve.wait_ge(silu_done, NB)
                    ins = v.tensor_tensor(o_i, o_i, gg[:, b, :], ALU.mult)
                ins.then_inc(gated, 1)

            def residual(b, n):
                dve.wait_ge(mix_part, 2 * b + n + 1)
                xs = x_sb[:, b, n * 512:(n + 1) * 512]
                mixed = bank[4 + n if b == NB - 1 else 6][:]
                v.scalar_tensor_tensor(out=xs, in0=xs, scalar=ALPHA, in1=mixed, op0=ALU.mult, op1=ALU.add).then_inc(mix_used, 1)
                dve.wait_ge(mix_used, 2 * b + n + 1)
                st(v.bn_stats(stats[:, n, :], xs))

            def copy_scores(h, u0):
                dve.wait_ge(sc_done, h + (u0 + 1))
                st(v.tensor_copy(sc, bank[7][:, 0:QW].rearrange("p (s n) -> p s n", s=2)))
                st.wait()
                dve.sem_inc(sc_copied, 1)

            def top16(*lists):
                st.wait()
                for src, _, vals, _ in lists:
                    st(v.max(vals[:, 0:8], src))
                st.wait()
                for src, src2, vals, where in lists:
                    st(v.max_index(where[:, 0:8], vals[:, 0:8], src))
                    st(v.match_replace(src2, vals[:, 0:8], src, LOWEST))
                st.wait()
                for _, src2, vals, _ in lists:
                    st(v.max(vals[:, 8:16], src2))
                st.wait()
                for _, src2, vals, where in lists:
                    st(v.max_index(where[:, 8:16], vals[:, 8:16], src2))

            halves = [(sc[:, s, :], sc2[:, s, :], top[:, s, :], topi[:, s, :]) for s in range(2)]

            def candidates(h, u0):
                st.wait()
                st(v.tensor_tensor(cand.rearrange("p (i j) -> p i j", i=TOPK),
                                   top[:, 0, :, None].to_broadcast([P, TOPK, TOPK]),
                                   top[:, 1, None, :].to_broadcast([P, TOPK, TOPK]), ALU.add))
                top16((cand, cand2, best, pos[:, 0, :]))
                st.wait()
                v.tensor_scalar(nbest, best[:, 0:1], -1.0, None, ALU.mult).then_inc(best_ready, 1)

            def finish_route(h, b, u0):
                par = (b % 2) * SLOTS

                def head_cols(h, par):
                    return slice(h * TOPK + par, (h + 1) * TOPK + par) if isinstance(h, int) else bass.ds(h * TOPK + par, TOPK)

                st(v.tensor_scalar(pos[:, 1, :], pos[:, 0, :], TOPK - 1, None, ALU.bitwise_and))
                st(v.tensor_copy(topf, topi[:]))
                st.wait()
                st(v.tensor_scalar(pos[:, 0, :], pos[:, 0, :], 4, None, ALU.logical_shift_right))
                st.wait()
                st(v.tensor_copy(posf, pos[:]))
                st.wait()
                st(v.tensor_tensor(onehot, posf[:, :, :, None].to_broadcast([P, 2, TOPK, TOPK]),
                                   iota16[:, None, None, :].to_broadcast([P, 2, TOPK, TOPK]), ALU.is_equal))
                st.wait()
                st(v.tensor_tensor(onehot, onehot, topf[:, :, None, :].to_broadcast([P, 2, TOPK, TOPK]), ALU.mult))
                st.wait()
                st(v.tensor_reduce(sel, onehot, AX_X, ALU.add))
                st.wait()
                st(v.scalar_tensor_tensor(out=idx[:, head_cols(h, par)], in0=sel[:, 0, :], scalar=float(NKEYS),
                                          in1=sel[:, 1, :], op0=ALU.mult, op1=ALU.add))
                dve.wait_ge(gexp, h + (u0 + 1))
                st(v.reciprocal(esum, esum))
                st.wait()
                st(v.tensor_scalar(gates[:, head_cols(h, par)], eb, esum, None, ALU.mult))
                st.wait()
                dve.sem_inc(routed, 1)

            for step, arg in plan:
                if step == "sp":
                    softplus(arg)
                elif step == "values_out" and arg == (NB - 1, 1):
                    dve.wait_ge(w_exp, NZ)
                    v.memset(zeros, 0.0).then_inc(filled, 1)
                elif step == "w":
                    if sb_tiles[arg][0] == sb_tiles[arg][2]:
                        diagonal_weights(arg)
                elif step == "mask_att":
                    mask_att(arg)
                elif step == "squares":
                    squares(*arg)
                elif step == "gate":
                    gate(*arg)
                elif step == "residual":
                    residual(*arg)
                elif step == "variance":
                    variance(var1)
                elif step == "normalise":
                    normalise(x_sb[:, arg, :], arg, rstd1, x1_ready)
                elif step == "copy_scores":
                    copy_scores(arg, 0)
                elif step == "top":
                    top16(*halves)
                elif step == "best":
                    candidates(arg, 0)
                elif step == "routed":
                    finish_route(arg, 0, 0)

            dve.sem_inc(w_done, 1)

            def dot(h, b, grp):
                for k in range(GROUP):
                    i = grp * GROUP + k
                    s = i % RING
                    dve.wait_ge(landed[s], h * (16 * TOPK // RING) + 16 * (b * SLOTS // RING + i // RING + 1))
                    u = rows[s][:, 0:D]
                    ins = v.tensor_tensor_reduce(u, u, x_sb[:, b, :], 1.0, 0.0, ALU.mult, ALU.add, dots[:, s:s + 1])
                ins.then_inc(dot_done, 1)

            def layer_norm(b):
                y = y2[b % 2]
                dve.wait_ge(v_done, RING + (b + 1) * SLOTS)
                if b == 0:
                    dve.wait_ge(ln2_in, 32)
                if b >= 2:
                    dve.wait_ge(stored[b % 2], 16 * (b // 2))
                for n in range(2):
                    st(v.scalar_tensor_tensor(out=y[:, n * 512:(n + 1) * 512], in0=x_sb[:, b, n * 512:(n + 1) * 512],
                                              scalar=ALPHA, in1=bank[2 * (b % 2) + n][:], op0=ALU.mult, op1=ALU.add))
                st.wait()
                dve.sem_inc(ffn_done, 1)
                for n in range(2):
                    st(v.bn_stats(stats[:, n, :], y[:, n * 512:(n + 1) * 512]))
                variance(var2)
                normalise(y, b, rstd2, y_ready)
                st.restart()

            def weigh(h, b, grp):
                dve.wait_ge(gelu_done, h * GROUPS + (b * PH * GROUPS + grp + 1))
                cols = group_cols(grp)
                v.tensor_tensor(wts[:, cols], acts[:, cols], gate_now[:, grp * GROUP:(grp + 1) * GROUP],
                                ALU.mult).then_inc(w_done, 1)

            st.restart()
            for b in range(NB):
                route = b < NB - 1
                u0 = (b + 1) * PH
                with dve.Fori(0, PH) as h:
                    for grp in range(GROUPS):
                        dot(h, b, grp)
                        if grp == 0:
                            dve.wait_ge(w_done, h * GROUPS + (b * PH * GROUPS + 1))
                            st(v.tensor_copy(gate_now, gates[:, bass.ds(h * TOPK + (b % 2) * SLOTS, TOPK)]))
                            st.wait()
                        weigh(h, b, grp)
                        if route and grp == 4:
                            copy_scores(h, u0)
                            top16(halves[0])
                        elif route and grp == 5:
                            top16(halves[1])
                        elif route and grp == 6:
                            candidates(h, u0)
                        elif route and grp == 7:
                            finish_route(h, b + 1, u0)
                    st.restart()
                for done in range(b - 1, b + (b == NB - 1)):
                    if done >= 0:
                        layer_norm(done)


def kernel(**inputs):
    import numpy as _np
    import concourse.bacc as _bacc
    from concourse import mybir as _mybir
    from concourse.bass_utils import run_bass_kernel_spmd as _run

    i = {k: _np.asarray(v) for k, v in inputs.items()}
    x = i["x"].reshape(512, 1024)
    laid = {
        "x": x,
        "xT": x.T,
        "w_in": i["w_in"][0],
        "w_gate": i["w_gla_gate"][0],
        "b_gate": i["b_gla_gate"].reshape(2, 128).T,
        "gains": _np.concatenate([i["gla_norm_g"].reshape(512), i["sb_norm_g"].reshape(512)]),
        "w_out": i["w_out"][0],
        "ln": _np.stack([i[k].reshape(1024) for k in ("ln1_g", "ln1_b", "ln2_g", "ln2_b")]),
        "w_query": i["peer_w_query"][0],
        "keysT": i["peer_sub_keys"].reshape(16, 128, 128).transpose(2, 0, 1).reshape(128, 2048),
        "experts": _np.concatenate([i["peer_u"][0], i["peer_v"][0]], axis=1),
    }
    nc = _bacc.Bacc("TRN2", target_bir_lowering=False, num_devices=1)
    arrays, args = {}, []
    for name, a in laid.items():
        a = _np.ascontiguousarray(a)
        arrays[f"in_{name}_dram"] = a
        args.append(nc.dram_tensor(f"in_{name}_dram", a.shape, _mybir.dt.from_np(a.dtype), kind="ExternalInput").ap())
    args.append(nc.dram_tensor("out_0_dram", (512, 1024), _mybir.dt.float32, kind="ExternalOutput").ap())
    hybrid_layer(nc, *args)
    r = _run(nc, [arrays], core_ids=[0])
    return r.results[0]["out_0_dram"].reshape(1, 512, 1024)
```
